# Optimizing a Trainium2 kernel written in Bass

```python
import jax, jax.numpy as jnp
from jax import lax
import numpy as np

D_MODEL = 1024
BATCH = 1
SEQ = 2048
DEPTH = 1

CHUNK = 64
EPS = 1e-6
GLA_HEADS = 4
GLA_DK = D_MODEL // 2 // GLA_HEADS
GLA_DV = D_MODEL // GLA_HEADS
GLA_RANK = 16
GLA_TAU = 16.0
SWA_HD = 64
SWA_HEADS = D_MODEL // SWA_HD
SWA_KV_HEADS = max(SWA_HEADS // 8, 1)
WINDOW = 128
WINDOW_CHUNKS = max(WINDOW // CHUNK, 1)
ROPE_THETA = 10000.0

GLA_QK = GLA_HEADS * GLA_DK
GLA_V = GLA_HEADS * GLA_DV
SWA_Q = SWA_HEADS * SWA_HD
SWA_KV = SWA_KV_HEADS * SWA_HD
SPLITS = (GLA_QK, GLA_QK, GLA_V, GLA_RANK, GLA_V, SWA_Q, SWA_KV, SWA_KV, SWA_Q, D_MODEL, D_MODEL)
D_IN = GLA_QK + GLA_QK + GLA_V + GLA_RANK + GLA_V + SWA_Q + SWA_KV + SWA_KV + SWA_Q + D_MODEL + D_MODEL

kernel_name = "hybrid_gla_swa_sink_gated_merge"

def rmsnorm(x, g):
    xf = x.astype(jnp.float32)
    y = xf * lax.rsqrt(jnp.mean(xf * xf, axis=-1, keepdims=True) + EPS)
    return (y * g.astype(jnp.float32)).astype(x.dtype)

def split_cols(t):
    out = []
    start = 0
    for w in SPLITS:
        out.append(t[..., start:start + w])
        start += w
    return out

def rope(x, positions):
    dh = x.shape[-1]
    half = dh // 2
    inv_freq = ROPE_THETA ** (-jnp.arange(half, dtype=jnp.float32) / half)
    ang = positions.astype(jnp.float32)[..., None] * inv_freq
    cos = jnp.cos(ang)[:, :, None, :]
    sin = jnp.sin(ang)[:, :, None, :]
    xf = x.astype(jnp.float32)
    x1, x2 = xf[..., :half], xf[..., half:]
    return jnp.concatenate([x1 * cos - x2 * sin, x2 * cos + x1 * sin], axis=-1).astype(x.dtype)

def gla_mixer(q, k, v, log_a):
    B, T, H, DK = q.shape
    DV = v.shape[-1]
    n_chunks = T // CHUNK

    def to_chunks(t):
        return jnp.moveaxis(t.astype(jnp.float32).reshape(B, n_chunks, CHUNK, H, t.shape[-1]), 1, 0)

    qc = to_chunks(q) * (DK ** -0.5)
    kc, vc, gc = to_chunks(k), to_chunks(v), to_chunks(log_a)

    def step(S, inp):
        q_, k_, v_, g_ = inp
        b = jnp.cumsum(g_, axis=1)
        b_last = b[:, -1]
        k_dec = k_ * jnp.exp(b_last[:, None] - b)
        S = S * jnp.exp(b_last)[..., None] + jnp.einsum('bchk,bchv->bhkv', k_dec, v_)
        o = jnp.einsum('bchk,bhkv->bchv', q_, S)
        return S, o

    S0 = jnp.zeros((B, H, DK, DV), jnp.float32)
    _, o = lax.scan(step, S0, (qc, kc, vc, gc))
    return jnp.moveaxis(o, 0, 1).reshape(B, T, H, DV)

def swa_sink_mixer(q, k, v, sinks):
    B, T, H, Dh = q.shape
    KV = k.shape[2]
    G = H // KV
    n_chunks = T // CHUNK
    qc = q.astype(jnp.float32).reshape(B, n_chunks, CHUNK, KV, G, Dh)
    kc = k.astype(jnp.float32).reshape(B, n_chunks, CHUNK, KV, Dh)
    vc = v.astype(jnp.float32).reshape(B, n_chunks, CHUNK, KV, Dh)

    def band(t):
        shifted = [jnp.pad(t, ((0, 0), (j, 0), (0, 0), (0, 0), (0, 0)))[:, :n_chunks]
                   for j in range(WINDOW_CHUNKS - 1, -1, -1)]
        return jnp.concatenate(shifted, axis=2)

    kb, vb = band(kc), band(vc)
    key_chunk = jnp.arange(n_chunks)[:, None] - jnp.arange(WINDOW_CHUNKS - 1, -1, -1)[None, :]
    valid = jnp.repeat(key_chunk >= 0, CHUNK, axis=1)
    s = jnp.einsum('bnqkgd,bnskd->bnkgqs', qc, kb) * (Dh ** -0.5)
    s = jnp.where(valid[None, :, None, None, None, :], s, -jnp.inf)
    sink = jnp.broadcast_to(sinks.astype(jnp.float32).reshape(1, 1, KV, G, 1, 1), s.shape[:-1] + (1,))
    p = jax.nn.softmax(jnp.concatenate([s, sink], axis=-1), axis=-1)[..., :-1]
    o = jnp.einsum('bnkgqs,bnskd->bnqkgd', p, vb)
    return o.reshape(B, T, H, Dh)

def setup_inputs(seed: int = 0) -> dict:
    key = jax.random.key(seed)
    ks = jax.random.split(key, 16)
    f32 = jnp.float32
    x = jax.random.normal(ks[0], (BATCH, SEQ, D_MODEL), f32)
    offset = jax.random.randint(ks[1], (BATCH, 1), 0, 4096, dtype=jnp.int32)
    positions = (offset + jnp.arange(SEQ, dtype=jnp.int32)[None, :]).astype(jnp.int32)
    g_pre = 1.0 + 0.02 * jax.random.normal(ks[2], (DEPTH, D_MODEL), f32)
    w_in = jax.random.normal(ks[3], (DEPTH, D_MODEL, D_IN), f32) * D_MODEL ** -0.5
    w_decay_up = jax.random.normal(ks[4], (DEPTH, GLA_RANK, GLA_QK), f32) * GLA_RANK ** -0.5
    b_decay_up = 0.1 * jax.random.normal(ks[5], (DEPTH, GLA_QK), f32)
    g_gla = 1.0 + 0.02 * jax.random.normal(ks[6], (DEPTH, GLA_HEADS, GLA_DV), f32)
    attn_sinks = 0.5 * jax.random.normal(ks[7], (DEPTH, SWA_HEADS), f32)
    w_branch_gla = jax.random.normal(ks[8], (DEPTH, GLA_V, D_MODEL), f32) * GLA_V ** -0.5
    w_branch_swa = jax.random.normal(ks[9], (DEPTH, SWA_Q, D_MODEL), f32) * SWA_Q ** -0.5
    b_merge = 0.02 * jax.random.normal(ks[10], (DEPTH, 2 * D_MODEL), f32)
    w_out = jax.random.normal(ks[11], (DEPTH, D_MODEL, D_MODEL), f32) * D_MODEL ** -0.5
    g_post = 1.0 + 0.02 * jax.random.normal(ks[12], (DEPTH, D_MODEL), f32)
    return {"x": x, "positions": positions, "g_pre": g_pre, "w_in": w_in,
            "w_decay_up": w_decay_up, "b_decay_up": b_decay_up, "g_gla": g_gla,
            "attn_sinks": attn_sinks, "w_branch_gla": w_branch_gla, "w_branch_swa": w_branch_swa,
            "b_merge": b_merge, "w_out": w_out, "g_post": g_post}

def reference(x, positions, g_pre, w_in, w_decay_up, b_decay_up, g_gla, attn_sinks,
              w_branch_gla, w_branch_swa, b_merge, w_out, g_post):
    B, T, _ = x.shape
    for layer in range(DEPTH):
        h = rmsnorm(x, g_pre[layer])
        proj = jnp.einsum('btd,de->bte', h, w_in[layer])
        (q_a, k_a, v_a, lr_a, z_a, q_b, k_b, v_b, z_b, m_a, m_b) = split_cols(proj)

        decay_logit = jnp.einsum('btr,rk->btk', lr_a, w_decay_up[layer]) + b_decay_up[layer]
        log_a = jax.nn.log_sigmoid(decay_logit.astype(jnp.float32)) / GLA_TAU
        o_a = gla_mixer(q_a.reshape(B, T, GLA_HEADS, GLA_DK), k_a.reshape(B, T, GLA_HEADS, GLA_DK),
                        v_a.reshape(B, T, GLA_HEADS, GLA_DV), log_a.reshape(B, T, GLA_HEADS, GLA_DK))
        o_a = rmsnorm(o_a, g_gla[layer]).reshape(B, T, GLA_V).astype(x.dtype) * jax.nn.silu(z_a)
        y_a = jnp.einsum('bte,ed->btd', o_a, w_branch_gla[layer])

        qb = rope(q_b.reshape(B, T, SWA_HEADS, SWA_HD), positions)
        kb = rope(k_b.reshape(B, T, SWA_KV_HEADS, SWA_HD), positions)
        o_b = swa_sink_mixer(qb, kb, v_b.reshape(B, T, SWA_KV_HEADS, SWA_HD), attn_sinks[layer])
        o_b = o_b.reshape(B, T, SWA_Q).astype(x.dtype) * jax.nn.silu(z_b)
        y_b = jnp.einsum('bte,ed->btd', o_b, w_branch_swa[layer])

        gate_a = jax.nn.sigmoid(m_a + b_merge[layer, :D_MODEL])
        gate_b = jax.nn.sigmoid(m_b + b_merge[layer, D_MODEL:])
        y = gate_a * y_a + gate_b * y_b
        out = jnp.einsum('btd,de->bte', y, w_out[layer])
        x = x + rmsnorm(out, g_post[layer])
    return x


_drawn_inputs = setup_inputs


def setup_inputs(seed=0):
    import zlib

    import numpy as np

    out = dict(_drawn_inputs(seed))
    spreads = {}
    factors = {'g_gla': 3.944, 'attn_sinks': 8.0, 'b_merge': 8.0, 'g_post': 4.081}
    for name, (base, spread) in spreads.items():
        noise = np.random.default_rng([zlib.crc32(name.encode()), seed]).standard_normal(out[name].shape)
        drawn = base * np.exp(spread * noise) if base else spread * noise
        out[name] = __import__('jax').numpy.asarray(drawn.astype(out[name].dtype))
    for name, factor in factors.items():
        out[name] = (out[name] * factor).astype(out[name].dtype)
    return out
```

```python
import numpy as np
import concourse.bass as bass
from concourse import mybir
from contextlib import ExitStack

P = 128
D = 1024
SEQ = 2048
TB = 512
NB = SEQ // TB
NT = TB // P
KD = D // P
CW = 256
HEADS_A, DK, DV = 4, 128, 256
CH = 64
HD = 64
GH = 8
RANK = 16
TAU = 16.0
EPS = 1e-6
NEG = -1e30

CHUNKS = ([("lr", 0), ("qA", 0), ("vA", 0), ("kA", 0), ("vA", 1), ("qA", 1), ("vA", 2), ("kA", 1),
           ("vA", 3), ("zA", 0), ("zA", 1), ("zA", 2), ("kvB", 0), ("qB", 0), ("qB", 1), ("zA", 3),
           ("qB", 2), ("qB", 3)]
          + [c for j in range(4) for c in (("mA", j), ("yA", j))]
          + [("zB", j) for j in range(4)]
          + [c for j in range(4) for c in (("mB", j), ("yB", j))]
          + [("out", j) for j in range(4)])
NC = len(CHUNKS)
TOKEN_MAJOR = ("kA", "vA", "kvB", "qB", "out")
UNITS = [(2 * c + j, kind, idx, j) for c, (kind, idx) in enumerate(CHUNKS) for j in range(2)
         if not (kind == "lr" and j)]
NU = len(UNITS)
SLOTS = 2 * NC
UNIT_AT = {u: (kind, idx, j) for u, kind, idx, j in UNITS}
FREED_BY_ACT = [u for u, kind, _, _ in UNITS if kind in ("lr", "mA", "mB", "out")]
FREED_BY_DVE = [u for u, kind, _, _ in UNITS if kind not in ("lr", "mA", "mB", "out")]
SCRATCH_USERS = [u for u, kind, _, _ in UNITS if kind in ("kA", "zA", "zB", "kvB", "qB")]
NEWTON = 3
NPB = 3

UNIT_LIST = [u for u, _, _, _ in UNITS]


def unit_no(u):
    return UNIT_LIST.index(u) + 1


def dve_no(u):
    return FREED_BY_DVE.index(u) + 1


def act_no(u):
    return FREED_BY_ACT.index(u) + 1


def scratch_no(u):
    return SCRATCH_USERS.index(u) + 1


def of_kind(*kinds):
    return [u for u, kind, _, _ in UNITS if kind in kinds]


Z_UNITS = of_kind("zA", "zB")
V_UNITS, Q_UNITS, K_UNITS = of_kind("vA"), of_kind("qA"), of_kind("kA")
M_UNITS, YB_UNITS = of_kind("mA", "mB"), of_kind("yB")
ROPE_UNITS = of_kind("kvB", "qB")
OUT_UNITS = of_kind("out")

LOGITS = {3 + t: t for t in range(NT)}
SUFFIX = {4 + t: t for t in range(NT)}
UPD = {8 + n: n for n in range(16)}
READ = {9 + n: n for n in range(16)}
NORM = {14 + 4 * h: h for h in range(HEADS_A)}
KTR = 28
QTR = {32 + 3 * s: s for s in range(8)}
SCORE = {33 + 3 * s: s for s in range(8)}
PTR = {35 + 3 * s: s for s in range(8)}
PV = {36 + 3 * s: s for s in range(8)}
XSTAT = {66 + t: t for t in range(NT)}
XRSTD = 70
XNORM = {71 + t: t for t in range(NT)}
XTR = {76 + g: (2 * g, 2 * g + 1) for g in range(4)}



def two_pi_parts(n):
    rest, parts = 2 * np.pi, []
    for _ in range(n - 1):
        unit = 2.0 ** (np.floor(np.log2(abs(rest))) - 6)
        part = float(np.round(rest / unit) * unit)
        parts.append(part)
        rest -= part
    return parts + [float(np.float32(rest))]


CONST_COLS = dict(ident=128, later=128, ones=128, pick=128, chunk_of=2, row16=1, one=1,
                  half_pi=1, inv_freq=32)


def const_array():
    c = {k: np.zeros((P, n), np.float32) for k, n in CONST_COLS.items()}
    r = np.arange(P)
    c["ident"][r, r] = 1
    c["later"][:] = (r[:, None] > r[None, :]) & (r[:, None] // CH == r[None, :] // CH)
    c["ones"][:] = 1
    c["pick"][0::CH, 0:CH] = 1
    c["chunk_of"][r, r // CH] = 1
    c["row16"][RANK] = 1
    c["one"][:] = 1
    c["half_pi"][:] = np.pi / 2
    c["inv_freq"][:] = (10000.0 ** (-np.arange(HD // 2) / (HD // 2))).astype(np.float32)
    return np.concatenate(list(c.values()), axis=1)


def mask_array():
    m = np.zeros((P, 4, 2, CH), np.float32)
    m[:, :, 1] = NEG
    return m.reshape(P, 4 * P)


class Count:

    def __init__(self, sem, per_block, unit=1, done_before=0):
        self.sem, self.per, self.unit, self.done_before = sem, per_block, unit, done_before

    def credit(self, eng):
        if self.per > self.done_before:
            eng.sem_inc(self.sem, (self.per - self.done_before) * self.unit)

    def at(self, i, n):
        return i * (self.per * self.unit) + (self.per + n) * self.unit


def build(nc, x, w, w_decay, pos, cols, sinks, gpost, consts, mask, out):
    f32, f32r, i32 = mybir.dt.float32, mybir.dt.float32r, mybir.dt.int32
    ALU, ACT, AX = mybir.AluOpType, mybir.ActivationFunctionType, mybir.AxisListType
    ds = bass.ds

    with ExitStack() as ctx:
        place = {"at": (nc.sbuf_base + 31) // 32 * 32}

        def region(nbytes):
            at = place["at"]
            place["at"] = at + nbytes
            return at

        def tile(name, shape, dt=f32, at=None):
            nbytes = 4 * int(np.prod(shape[1:]))
            return nc.alloc_sbuf_tensor_at(name, list(shape), dt,
                                           offset=region((nbytes + 31) // 32 * 32) if at is None else at)

        h_hi = tile("h_hi", [P, KD, TB], f32r)
        h_lo = tile("h_lo", [P, KD, TB], f32r)
        w_raw = [tile(f"w_raw{s}", [P, KD // 2, CW]) for s in range(2)]
        w_hi = [tile(f"w_hi{s}", [P, KD, CW], f32r) for s in range(2)]
        w_lo = [tile(f"w_lo{s}", [P, KD, CW], f32r) for s in range(2)]
        at = region(2 * KD * TB * 4)
        g_hi = tile("g_hi", [P, KD, TB], f32r, at)
        g_lo = tile("g_lo", [P, KD, TB], f32r, at + KD * TB * 4)
        x_res = tile("x_res", [P, NT, D], f32, at)
        K1 = 1024
        at = region(40 * K1)
        v_hi = [tile(f"v_hi{s}", [P, NT, DV], f32r, at + 4 * K1 * s) for s in range(2)]
        v_lo = [tile(f"v_lo{s}", [P, NT, DV], f32r, at + (8 + 4 * s) * K1) for s in range(2)]
        q_hi = [tile(f"q_hi{s}", [P, 2, TB], f32r, at + (16 + 4 * s) * K1) for s in range(2)]
        q_lo = [tile(f"q_lo{s}", [P, 2, TB], f32r, at + (24 + 4 * s) * K1) for s in range(2)]
        kd_hi = tile("kd_hi", [P, NT, 2 * DK], f32r, at + 32 * K1)
        kd_lo = tile("kd_lo", [P, NT, 2 * DK], f32r, at + 36 * K1)
        q_rope = tile("q_rope", [P, NT, D], f32, at)
        ob = tile("ob", [P, KD, TB], f32, at + 16 * K1)
        y_hi = tile("y_hi", [P, KD, TB], f32r, at)
        y_lo = tile("y_lo", [P, KD, TB], f32r, at + 16 * K1)
        at = region(KD * TB * 4)
        oa = tile("oa", [P, KD, TB], f32, at)
        y_sum = tile("y_sum", [P, KD, TB], f32, at)
        rows = tile("rows", [P, NT, D], f32, at)
        at = region(16 * K1)
        decay_w = tile("decay_w", [P, NT, HEADS_A * DK], f32, at)
        s_hi = tile("s_hi", [P, 2, DV], f32r, at + 8 * K1)
        s_lo = tile("s_lo", [P, 2, DV], f32r, at + 10 * K1)
        s_mid = tile("s_mid", [P, DV], f32, at + 12 * K1)
        k_rope = tile("k_rope", [P, NT, 2, 2, HD], f32, at)
        prob = [tile(f"prob{s}", [P, GH, P], f32, at + 4 * K1 * s) for s in range(2)]
        prob_t = tile("prob_t", [P, GH, P], f32, at + 8 * K1)
        q_t = [tile(f"q_t{s}", [P, NT, P], f32, at + (12 + 2 * s) * K1) for s in range(2)]
        x_in = tile("x_in", [P, NT, D], f32, at)
        at = region(8 * K1)
        gate = [tile(f"gate{s}", [P, TB], f32, at + 2 * K1 * s) for s in range(4)]
        soft = tile("soft", [P, TB], f32, at)
        log_a = [tile(f"log_a{s}", [P, TB], f32, at + (2 + 2 * s) * K1) for s in range(2)]
        lr_t = tile("lr_t", [P, TB], f32, at + 6 * K1)
        square = [tile(f"square{s}", [P, TB], f32, at + 2 * K1 * s) for s in range(2)]
        mean_a = tile("mean_a", [P, TB], f32, at + 4 * K1)
        rstd_a = tile("rstd_a", [P, TB], f32, at + 6 * K1)
        at = region(8 * K1)
        scratch = [[tile(f"scratch{s}{j}", [P, TB], f32, at + (4 * s + 2 * j) * K1) for j in range(2)]
                   for s in range(2)]
        pos_i = tile("pos_i", [P, NB * NT], i32, at + 6 * K1)
        pos_f = tile("pos_f", [P, NB * NT], f32, at + 7 * K1)
        state = tile("state", [P, HEADS_A, DV])
        k_odd = tile("k_odd", [P, 2, NT, P])
        k_even = tile("k_even", [P, 2, NT, P])
        v_odd = tile("v_odd", [P, NT, P])
        v_even = tile("v_even", [P, NT, P])
        cos = tile("cos", [P, NB * NT, HD // 2])
        sin = tile("sin", [P, NB * NT, HD // 2])
        gpost_sb = tile("gpost_sb", [P, D])
        wdecay_sb = tile("wdecay_sb", [32, HEADS_A * DK])
        const_sb = tile("const_sb", [P, sum(CONST_COLS.values())])
        cols_sb = tile("cols_sb", [P, 32])
        half_bm = tile("half_bm", [P, 16])
        sink_sb = tile("sink_sb", [P, 16])
        mask_sb = tile("mask_sb", [P, 4 * P])
        decay_s = tile("decay_s", [P, NT, HEADS_A, 2])
        top = [tile(f"top{s}", [P, GH]) for s in range(2)]
        sink_e = [tile(f"sink_e{s}", [P, GH]) for s in range(2)]
        den = [tile(f"den{s}", [P, GH]) for s in range(2)]
        x_stat = o_stat = tile("row_stat", [P, NT, 2, 6])
        x_sm = o_sm = tile("row_terms", [P, 10, NT])
        ang, turns = scratch[0]
        r_abs = scratch[1][0]

        cs, col = {}, 0
        for name, n in CONST_COLS.items():
            cs[name] = const_sb[:, col:col + n]
            col += n

        pu = [ctx.enter_context(nc.psum_tensor(f"pu{b}", [P, TB], f32)) for b in range(NPB)]
        pm = [ctx.enter_context(nc.psum_tensor(f"pm{b}", [P, TB], f32)) for b in range(5)]

        def count(name, per, unit=1, done_before=0):
            return Count(ctx.enter_context(nc.semaphore(name)), per, unit, done_before)

        def plain(name):
            return ctx.enter_context(nc.semaphore(name))

        const_in = plain("const_in")
        raw_in = [count(f"raw_in{h}", NC, 16, 2) for h in range(2)]
        x_in_ok = count("x_in_ok", NT, 16, NT)
        x_res_ok = count("x_res_ok", NT, 16)
        stored = count("stored", NT, 16, NT)
        unit_done = count("unit_done", NU)
        logits_ok = count("logits_ok", NT)
        suffix_ok = count("suffix_ok", NT)
        upd_ok = count("upd_ok", 16)
        read_ok = count("read_ok", 16)
        ssq_ok = count("ssq_ok", HEADS_A)
        ktr_ok = count("ktr_ok", 2)
        qtr_ok = count("qtr_ok", 8)
        score_ok = count("score_ok", 8)
        ptr_ok = count("ptr_ok", 8)
        pv_ok = count("pv_ok", 8)
        xtr_ok = count("xtr_ok", KD, done_before=KD)
        w_hi_ok = count("w_hi_ok", 2 * NC, done_before=4)
        freed_act = count("freed_act", len(FREED_BY_ACT))
        act_seq = count("act_seq", 2 * NT + HEADS_A)
        softplus_ok = count("softplus_ok", NT)
        decay_ok = count("decay_ok", NT + 1)
        v_hi_ok = count("v_hi_ok", len(V_UNITS))
        q_hi_ok = count("q_hi_ok", len(Q_UNITS))
        kd_hi_ok = count("kd_hi_ok", len(K_UNITS))
        s_hi_ok = count("s_hi_ok", 32)
        oa_ok = count("oa_ok", 4 * HEADS_A)
        rstd_a0_ok = count("rstd_a0_ok", HEADS_A)
        z_tanh_ok = count("z_tanh_ok", len(Z_UNITS))
        g_hi_ok = count("g_hi_ok", len(Z_UNITS))
        k_odd_ok = count("k_odd_ok", 2)
        q_t_ok = count("q_t_ok", 8)
        p_exp_ok = count("p_exp_ok", 16)
        pt_even_ok = count("pt_even_ok", 8)
        ob_ok = count("ob_ok", 8)
        y_hi_ok = count("y_hi_ok", KD)
        h_hi_ok = count("h_hi_ok", KD, done_before=KD)
        trig_ok = plain("trig_ok")
        freed_dve = count("freed_dve", len(FREED_BY_DVE))
        ROW_LINKS = 2 * NT + 4 + 2 + 3 * NEWTON
        dve_seq = count("dve_seq", 2 * ROW_LINKS + 3 * HEADS_A + 2 + 4 * 8, done_before=ROW_LINKS + 1)
        log_a_ok = count("log_a_ok", NT)
        state_ok = count("state_ok", 32)
        mean_a_ok = count("mean_a_ok", HEADS_A)
        oa_norm_ok = count("oa_norm_ok", 2 * HEADS_A)
        gated_ok = count("gated_ok", len(Z_UNITS))
        k_even_ok = count("k_even_ok", 3)
        v_even_ok = count("v_even_ok", 1)
        shift_ok = count("shift_ok", 8)
        sink_d_ok = count("sink_d_ok", 8)
        den0_ok = count("den0_ok", 8)
        den_ok = count("den_ok", 8)
        pt_odd_ok = count("pt_odd_ok", 8)
        x_norm_ok = count("x_norm_ok", NT, done_before=NT)
        y_sum_ok = count("y_sum_ok", KD)
        o_scaled_ok = count("o_scaled_ok", NT)
        o_dve_ok = count("o_dve_ok", 2)
        h_lo_ok = count("h_lo_ok", KD, done_before=KD)
        prep_ok = plain("prep_ok")
        w_lo_ok = count("w_lo_ok", 2 * NC, done_before=4)
        scratch_free = count("scratch_free", len(SCRATCH_USERS))
        s_lo_ok = count("s_lo_ok", 32)
        p_norm_ok = count("p_norm_ok", 8)
        y_lo_ok = count("y_lo_ok", KD)
        o_pool_ok = count("o_pool_ok", 2)
        zeroed = plain("zeroed")

        ACT_COUNTS = [w_hi_ok, freed_act, act_seq, softplus_ok, decay_ok, v_hi_ok, q_hi_ok, kd_hi_ok,
                      s_hi_ok, oa_ok, rstd_a0_ok, z_tanh_ok, g_hi_ok, k_odd_ok, q_t_ok, p_exp_ok,
                      pt_even_ok, ob_ok, y_hi_ok, h_hi_ok]
        DVE_COUNTS = [freed_dve, dve_seq, log_a_ok, state_ok, mean_a_ok, oa_norm_ok, gated_ok,
                      k_even_ok, v_even_ok, shift_ok, sink_d_ok, den0_ok, den_ok, pt_odd_ok,
                      x_norm_ok, y_sum_ok, o_scaled_ok, o_dve_ok, h_lo_ok]
        PE_COUNTS = [unit_done, logits_ok, suffix_ok, upd_ok, read_ok, ssq_ok, ktr_ok, qtr_ok,
                     score_ok, ptr_ok, pv_ok, xtr_ok]
        POOL_COUNTS = [w_lo_ok, scratch_free, s_lo_ok, p_norm_ok, y_lo_ok, o_pool_ok, stored]
        SP_COUNTS = raw_in + [x_in_ok, x_res_ok]

        def w_half_no(c, half):
            return 2 * c + half - 3

        def as_f32(ap):
            return ap.bitcast(f32)

        block = ctx.enter_context(nc.Block())

        @block.sync
        def _(sp):
            for c in SP_COUNTS:
                c.credit(sp)

            def load_w(c, half):
                sp.dma_start(w_raw[half][:, :, :], w[c, :, half * (KD // 2):(half + 1) * (KD // 2), :]) \
                  .then_inc(raw_in[half].sem, 16)

            def load_x(dst, at, c):
                for t in range(NT):
                    sp.dma_start(dst[:, t, :], x[ds(at + t * P, P), :]).then_inc(c.sem, 16)

            load_x(x_in, 0, x_in_ok)
            for dst, src in ((const_sb, consts), (cols_sb, cols)):
                sp.dma_start(dst[:, :], src).then_inc(const_in, 16)
            for half in range(2):
                load_w(0, half)
            sp.dma_start(mask_sb[:, :], mask).then_inc(const_in, 16)
            for half in range(2):
                sp.wait_ge(w_lo_ok.sem, w_lo_ok.at(-1, w_half_no(NC, half)))
                load_w(1, half)
            with sp.Fori(0, NB) as i:
                for c in range(2, NC + 2):
                    for half in range(2):
                        sp.wait_ge(w_lo_ok.sem, w_lo_ok.at(i, w_half_no(c - 1, half)))
                        load_w(c % NC, half)
                    if c == 32:
                        sp.wait_ge(pv_ok.sem, pv_ok.at(i, 8))
                        load_x(x_in, ((i + 1) % NB) * TB, x_in_ok)
                    if c == 39:
                        sp.wait_ge(unit_done.sem, unit_done.at(i, unit_no(75)))
                        load_x(x_res, i * TB, x_res_ok)
            for c in raw_in + [x_in_ok, x_res_ok, stored]:
                sp.wait_ge(c.sem, c.at(NB - 1, c.per))

        @block.tensor
        def _(pe):
            for c in PE_COUNTS:
                c.credit(pe)
            mm, tr = nc.tensor.matmul, nc.tensor.transpose

            def passes(a_hi, a_lo, b_hi, b_lo):
                return ((a_hi, b_hi), (a_hi, b_lo), (a_lo, b_hi))

            def x_transpose(i, k):
                if k >= 4:
                    pe.wait_ge(h_lo_ok.sem, h_lo_ok.at(i, k - 3))
                for t in range(NT):
                    last = tr(pm[k % 4][:, t * P:(t + 1) * P], x_in[:, t, k * P:(k + 1) * P], cs["ident"])
                last.then_inc(xtr_ok.sem, 1)

            def unit(i, u):
                kind, idx, j = UNIT_AT[u]
                c = u // 2
                bank = pu[u % NPB]
                if j == 0:
                    pe.wait_ge(w_lo_ok.sem, w_lo_ok.at(i, w_half_no(c, 1)))
                if u == 0:
                    pe.wait_ge(h_lo_ok.sem, h_lo_ok.at(i, 0))
                prev = u - NPB
                if prev == 1:
                    prev = 1 - NPB
                back = prev < 0
                prev %= SLOTS
                own, c_free = ((FREED_BY_ACT, freed_act) if prev in FREED_BY_ACT
                               else (FREED_BY_DVE, freed_dve))
                pe.wait_ge(c_free.sem, c_free.at(i, own.index(prev) + 1 - (len(own) if back else 0)))
                if kind in ("yA", "yB"):
                    if idx == 0 and j == 0:
                        pe.wait_ge(scratch_free.sem, scratch_free.at(i, scratch_no(31 if kind == "yA" else 59)))
                    a_hi, a_lo = g_hi, g_lo
                elif kind == "out":
                    a_hi, a_lo = y_hi, y_lo
                else:
                    a_hi, a_lo = h_hi, h_lo
                wh, wl = w_hi[c % 2], w_lo[c % 2]
                if kind in TOKEN_MAJOR:
                    for t in (2 * j, 2 * j + 1):
                        for k in range(KD):
                            if u == OUT_UNITS[0] and t == 0:
                                pe.wait_ge(y_lo_ok.sem, y_lo_ok.at(i, k + 1))
                            for n, (a, b) in enumerate(passes(a_hi, a_lo, wh, wl)):
                                last = mm(bank[:, (t % 2) * CW:(t % 2 + 1) * CW],
                                          a[:, k, t * P:(t + 1) * P], b[:, k, :],
                                          start=(k == 0 and n == 0), stop=(k == KD - 1 and n == 2))
                else:
                    for k in range(KD):
                        for n, (b, a) in enumerate(passes(wh, wl, a_hi, a_lo)):
                            last = mm(bank[:, :], b[:, k, j * P:(j + 1) * P], a[:, k, :],
                                      start=(k == 0 and n == 0), stop=(k == KD - 1 and n == 2))
                last.then_inc(unit_done.sem, 1)

            def logits(i, t):
                pe.wait_ge(freed_act.sem, freed_act.at(i, 1))
                if t:
                    pe.wait_ge(log_a_ok.sem, log_a_ok.at(i, t))
                mm(pm[0][:, :], lr_t[0:32, t * P:(t + 1) * P], wdecay_sb[:, :],
                   start=True, stop=True).then_inc(logits_ok.sem, 1)

            def suffix(i, t):
                pe.wait_ge(log_a_ok.sem, log_a_ok.at(i, t + 1))
                if t:
                    pe.wait_ge(decay_ok.sem, decay_ok.at(i, t))
                g = log_a[t % 2]
                mm(pm[1][:, :], cs["later"], g[:, :], start=True, stop=True)
                for h in range(HEADS_A):
                    o = (t * HEADS_A + h) * 2
                    last = mm(pm[2][:, o:o + 2], g[:, h * DK:(h + 1) * DK], cs["chunk_of"],
                              start=True, stop=True)
                last.then_inc(suffix_ok.sem, 1)

            def update(i, n):
                h, t = divmod(n, NT)
                if t % 2 == 0:
                    pe.wait_ge(freed_dve.sem, freed_dve.at(i, dve_no(V_UNITS[2 * h + t // 2])))
                    pe.wait_ge(scratch_free.sem, scratch_free.at(i, scratch_no(K_UNITS[2 * (h // 2) + t // 2])))
                if n == 0:
                    pe.wait_ge(decay_ok.sem, decay_ok.at(i, NT + 1))
                else:
                    pe.wait_ge(state_ok.sem, state_ok.at(i, 2 * n))
                for c in range(2):
                    r = slice(c * CH, (c + 1) * CH)
                    for m, (a, b) in enumerate(passes(kd_hi, kd_lo, v_hi[h % 2], v_lo[h % 2])):
                        last = mm(pm[c][:, 0:DV], a[r, t, (h % 2) * DK:(h % 2 + 1) * DK], b[r, t, :],
                                  start=(m == 0), stop=(m == 2))
                last.then_inc(upd_ok.sem, 1)

            def read_state(i, n):
                h, t = divmod(n, NT)
                pe.wait_ge(s_lo_ok.sem, s_lo_ok.at(i, 2 * n + 2))
                if t == 0:
                    pe.wait_ge(freed_dve.sem, freed_dve.at(i, dve_no(Q_UNITS[h])))
                    if h:
                        pe.wait_ge(oa_ok.sem, oa_ok.at(i, 4 * h))
                for c in range(2):
                    tok = slice(t * P + c * CH, t * P + (c + 1) * CH)
                    for j in range(2):
                        for m, (a, b) in enumerate(passes(s_hi, s_lo, q_hi[h // 2], q_lo[h // 2])):
                            last = mm(pm[2 + j][:, tok], a[:, c, j * P:(j + 1) * P], b[:, h % 2, tok],
                                      start=(m == 0), stop=(m == 2))
                last.then_inc(read_ok.sem, 1)

            def norm_sums(i, h):
                pe.wait_ge(oa_ok.sem, oa_ok.at(i, 4 * h + 4))
                if h:
                    pe.wait_ge(mean_a_ok.sem, mean_a_ok.at(i, h))
                for j in range(2):
                    last = mm(pm[4][:, :], cs["ones"], square[j][:, :], start=(j == 0), stop=(j == 1))
                last.then_inc(ssq_ok.sem, 1)

            def k_transpose(i):
                pe.wait_ge(scratch_free.sem, scratch_free.at(i, scratch_no(25)))
                pe.wait_ge(state_ok.sem, state_ok.at(i, 32))
                for g in range(2):
                    for t in range(NT):
                        last = tr(pm[g][:, t * P:(t + 1) * P],
                                  k_rope[:, t, g, :, :].rearrange("p a b -> p (a b)"), cs["ident"])
                    last.then_inc(ktr_ok.sem, 1)

            def q_transpose(i, s):
                g, t = divmod(s, NT)
                if t == 0:
                    pe.wait_ge(scratch_free.sem, scratch_free.at(i, scratch_no(29 + 6 * g)))
                if s == 0:
                    pe.wait_ge(mean_a_ok.sem, mean_a_ok.at(i, HEADS_A))
                else:
                    pe.wait_ge(q_t_ok.sem, q_t_ok.at(i, s))
                for e in range(4):
                    last = tr(pm[4][:, e * P:(e + 1) * P],
                              q_rope[:, t, (4 * g + e) * P:(4 * g + e + 1) * P], cs["ident"])
                last.then_inc(qtr_ok.sem, 1)

            def scores_wait(i, s):
                t = s % NT
                pe.wait_ge(q_t_ok.sem, q_t_ok.at(i, s + 1))
                if t == 0:
                    pe.wait_ge(shift_ok.sem, shift_ok.at(i, s))
                if s == 0:
                    pe.wait_ge(k_even_ok.sem, k_even_ok.at(i, 3))
                    pe.wait_ge(k_odd_ok.sem, k_odd_ok.at(i, 2))
                    pe.wait_ge(oa_ok.sem, oa_ok.at(i, 16))
                else:
                    pe.wait_ge(pt_even_ok.sem, pt_even_ok.at(i, s))
                    pe.wait_ge(pt_odd_ok.sem, pt_odd_ok.at(i, s))

            def scores(i, s):
                g, t = divmod(s, NT)
                q = q_t[s % 2]
                for par in range(2):
                    dims = slice(par * HD, (par + 1) * HD)
                    if t == 0:
                        mm(pm[1 + par][:, :], cs["pick"][dims, :], mask_sb[dims, :], start=True, stop=False)
                    for c, keys in enumerate((k_even, k_odd)):
                        rows_ = slice(c * CH, (c + 1) * CH)
                        for e in range(4):
                            last = mm(pm[1 + par][rows_, e * P:(e + 1) * P],
                                      q[dims, e, rows_], keys[dims, g, t, :],
                                      start=t > 0, stop=t > 0 or e == 3)
                last.then_inc(score_ok.sem, 1)

            def p_transpose(i, s):
                pe.wait_ge(p_norm_ok.sem, p_norm_ok.at(i, s + 1))
                for hh in range(GH):
                    last = tr(pm[1 + hh // 4][:, (hh % 4) * P:(hh % 4 + 1) * P],
                              prob[s % 2][:, hh, :], cs["ident"])
                last.then_inc(ptr_ok.sem, 1)

            def p_times_v(i, s):
                g, t = divmod(s, NT)
                pe.wait_ge(pt_even_ok.sem, pt_even_ok.at(i, s + 1))
                pe.wait_ge(pt_odd_ok.sem, pt_odd_ok.at(i, s + 1))
                if s == 0:
                    pe.wait_ge(v_even_ok.sem, v_even_ok.at(i, 1))
                else:
                    pe.wait_ge(ob_ok.sem, ob_ok.at(i, s))
                for par in range(2):
                    for c, v in enumerate((v_even, v_odd)):
                        o = pm[3][par * HD:(par + 1) * HD, :].rearrange("p (e q) -> p e q", e=4)
                        last = mm(o[:, :, c * CH:(c + 1) * CH], v[:, t, g * HD:(g + 1) * HD],
                                  prob_t[:, par * 4:(par + 1) * 4, c * CH:(c + 1) * CH],
                                  start=True, stop=True)
                last.then_inc(pv_ok.sem, 1)

            pe.wait_ge(const_in, 48)
            pe.wait_ge(x_norm_ok.sem, x_norm_ok.at(-1, NT))
            for k in range(KD):
                x_transpose(-1, k)
            pe.wait_ge(zeroed, 3)
            pe.wait_ge(stored.sem, stored.at(-1, NT))
            with pe.Fori(0, NB) as i:
                for u in range(SLOTS):
                    if u in LOGITS:
                        logits(i, LOGITS[u])
                    if u in SUFFIX:
                        suffix(i, SUFFIX[u])
                    if u in UPD:
                        update(i, UPD[u])
                    if u in READ:
                        read_state(i, READ[u])
                    if u in NORM:
                        norm_sums(i, NORM[u])
                    if u == KTR:
                        k_transpose(i)
                    if u in PTR:
                        p_transpose(i, PTR[u])
                    if u in QTR:
                        q_transpose(i, QTR[u])
                    if u in SCORE:
                        scores_wait(i, SCORE[u])
                    if u in PV:
                        p_times_v(i, PV[u])
                    if u in SCORE:
                        scores(i, SCORE[u])
                    if u in XTR:
                        if XTR[u][0] == 0:
                            pe.wait_ge(x_norm_ok.sem, x_norm_ok.at(i, NT))
                            pe.wait_ge(ob_ok.sem, ob_ok.at(i, 8))
                        for k in XTR[u]:
                            x_transpose(i, k)
                    if u in UNIT_AT:
                        unit(i, u)

        @block.scalar
        def _(act):
            for c in ACT_COUNTS:
                c.credit(act)
            A = nc.scalar.activation
            seq = {"n": 0}

            def link(i, ins):
                seq["n"] += 1
                ins.then_inc(act_seq.sem, 1)
                act.wait_ge(act_seq.sem, act_seq.at(i, seq["n"]))

            def split_w(i, c, half):
                act.wait_ge(raw_in[half].sem, raw_in[half].at(i, c - 1))
                act.wait_ge(unit_done.sem, unit_done.at(i, unit_no(2 * c - 3) if c > 2 else c - 1))
                ks = slice(half * (KD // 2), (half + 1) * (KD // 2))
                A(w_hi[c % 2][:, ks, :], w_raw[half][:, :, :], ACT.Copy).then_inc(w_hi_ok.sem, 1)

            def x_split(i, k):
                act.wait_ge(xtr_ok.sem, xtr_ok.at(i, k + 1))
                A(h_hi[:, k, :], pm[k % 4][:, :], ACT.Copy, scale=cols_sb[:, k:k + 1]) \
                    .then_inc(h_hi_ok.sem, 1)

            for c in (NC, NC + 1):
                for half in range(2):
                    split_w(-1, c, half)
            act.wait_ge(const_in, 48)
            for k in range(KD):
                x_split(-1, k)
            act.wait_ge(prep_ok, ROPE_PREP)
            A(sin[:, :, :].rearrange("p a b -> p (a b)"), ang[:, :], ACT.Sin).then_inc(trig_ok, 1)
            A(cos[:, :, :].rearrange("p a b -> p (a b)"), r_abs[:, :], ACT.Sin, scale=-1.0,
              bias=cs["half_pi"]).then_inc(trig_ok, 1)

            with act.Fori(0, NB) as i:
                seq["n"] = 0
                for u in range(SLOTS):
                    if u >= 2:
                        split_w(i, u // 2 + 1, u % 2)
                    if u in LOGITS:
                        t = LOGITS[u]
                        act.wait_ge(logits_ok.sem, logits_ok.at(i, t + 1))
                        if t:
                            act.wait_ge(log_a_ok.sem, log_a_ok.at(i, t))
                        link(i, A(soft[:, :], pm[0][:, :], ACT.Abs))
                        link(i, A(soft[:, :], soft[:, :], ACT.Exp, scale=-1.0))
                        A(soft[:, :], soft[:, :], ACT.Ln, bias=cs["one"]).then_inc(softplus_ok.sem, 1)
                    if u in SUFFIX:
                        t = SUFFIX[u]
                        act.wait_ge(suffix_ok.sem, suffix_ok.at(i, t + 1))
                        A(decay_w[:, t, :], pm[1][:, :], ACT.Exp, scale=1.0 / TAU) \
                            .then_inc(decay_ok.sem, 1)
                        if t == NT - 1:
                            A(decay_s[:, :, :, :].rearrange("p a b c -> p (a b c)"),
                              pm[2][:, 0:NT * HEADS_A * 2], ACT.Exp, scale=1.0 / TAU) \
                                .then_inc(decay_ok.sem, 1)
                    if u in UPD:
                        n = UPD[u]
                        act.wait_ge(read_ok.sem, read_ok.at(i, n))
                        for c in range(2):
                            act.wait_ge(state_ok.sem, state_ok.at(i, 2 * n + c + 1))
                            src = s_mid[:, :] if c == 0 else state[:, n // NT, :]
                            A(s_hi[:, c, :], src, ACT.Copy).then_inc(s_hi_ok.sem, 1)
                    if u in READ and READ[u] % NT == NT - 1:
                        h = READ[u] // NT
                        act.wait_ge(read_ok.sem, read_ok.at(i, READ[u] + 1))
                        if h == 0:
                            act.wait_ge(stored.sem, stored.at(i, 0))
                        else:
                            act.wait_ge(oa_norm_ok.sem, oa_norm_ok.at(i, 2 * h))
                        for j in range(2):
                            A(oa[:, 2 * h + j, :], pm[2 + j][:, :], ACT.Copy).then_inc(oa_ok.sem, 1)
                            A(square[j][:, :], pm[2 + j][:, :], ACT.Square).then_inc(oa_ok.sem, 1)
                    if u in NORM:
                        h = NORM[u]
                        act.wait_ge(mean_a_ok.sem, mean_a_ok.at(i, h + 1))
                        link(i, A(rstd_a[:, :], mean_a[:, :], ACT.Ln))
                        A(rstd_a[:, :], rstd_a[:, :], ACT.Exp, scale=-0.5).then_inc(rstd_a0_ok.sem, 1)
                    if u == KTR:
                        for g in range(2):
                            act.wait_ge(ktr_ok.sem, ktr_ok.at(i, g + 1))
                            if g == 0:
                                act.wait_ge(k_even_ok.sem, k_even_ok.at(i, 1))
                            A(k_odd[:, g, :, :].rearrange("p a b -> p (a b)"), pm[g][:, :], ACT.Copy) \
                                .then_inc(k_odd_ok.sem, 1)
                    if u in PTR:
                        s = PTR[u]
                        act.wait_ge(ptr_ok.sem, ptr_ok.at(i, s + 1))
                        act.wait_ge(pv_ok.sem, pv_ok.at(i, s))
                        A(prob_t[:, 0:4, :].rearrange("p a b -> p (a b)"), pm[1][:, :], ACT.Copy) \
                            .then_inc(pt_even_ok.sem, 1)
                    if u in QTR:
                        s = QTR[u]
                        act.wait_ge(qtr_ok.sem, qtr_ok.at(i, s + 1))
                        if s >= 2:
                            act.wait_ge(score_ok.sem, score_ok.at(i, s - 1))
                        A(q_t[s % 2][:, :, :].rearrange("p a b -> p (a b)"), pm[4][:, :], ACT.Copy) \
                            .then_inc(q_t_ok.sem, 1)
                    if u in PV:
                        s = PV[u]
                        g, t = divmod(s, NT)
                        act.wait_ge(pv_ok.sem, pv_ok.at(i, s + 1))
                        A(ob[:, 4 * g:4 * g + 4, t * P:(t + 1) * P],
                          pm[3][:, :].rearrange("p (e q) -> p e q", e=4), ACT.Copy).then_inc(ob_ok.sem, 1)
                    if u in SCORE:
                        s = SCORE[u]
                        act.wait_ge(shift_ok.sem, shift_ok.at(i, s + 1))
                        A(prob[s % 2][:, :, :], prob[s % 2][:, :, :], ACT.Exp).then_inc(p_exp_ok.sem, 1)
                        act.wait_ge(sink_d_ok.sem, sink_d_ok.at(i, s + 1))
                        A(sink_e[s % 2][:, :], sink_e[s % 2][:, :], ACT.Exp).then_inc(p_exp_ok.sem, 1)
                    if u in XTR:
                        for k in XTR[u]:
                            x_split(i, k)
                    if u - 1 in Z_UNITS:
                        _, idx, j = UNIT_AT[u - 1]
                        act.wait_ge(gated_ok.sem, gated_ok.at(i, Z_UNITS.index(u - 1) + 1))
                        A(g_hi[:, 2 * idx + j, :], scratch[SCRATCH_USERS.index(u - 1) % 2][0][:, :],
                          ACT.Copy).then_inc(g_hi_ok.sem, 1)
                    if u not in UNIT_AT:
                        continue
                    kind, idx, j = UNIT_AT[u]
                    bank = pu[u % NPB]
                    if kind in ("kA", "zA", "zB"):
                        pair = scratch[SCRATCH_USERS.index(u) % 2]
                    if kind != "kA" and kind not in ("yA", "yB", "kvB", "qB"):
                        act.wait_ge(unit_done.sem, unit_done.at(i, unit_no(u)))
                    if kind == "lr":
                        A(lr_t[0:32, :], bank[0:32, :], ACT.Identity, bias=cs["row16"][0:32, :]) \
                            .then_inc(freed_act.sem, 1)
                    elif kind == "vA":
                        A(v_hi[idx % 2][:, 2 * j:2 * j + 2, :].rearrange("p a b -> p (a b)"), bank[:, :],
                          ACT.Copy).then_inc(v_hi_ok.sem, 1)
                    elif kind == "qA":
                        A(q_hi[idx][:, j, :], bank[:, :], ACT.Copy, scale=DK ** -0.5) \
                            .then_inc(q_hi_ok.sem, 1)
                    elif kind == "kA":
                        act.wait_ge(freed_dve.sem, freed_dve.at(i, dve_no(u)))
                        if idx:
                            act.wait_ge(upd_ok.sem, upd_ok.at(i, 2 * (j + 1) + NT))
                        A(kd_hi[:, 2 * j:2 * j + 2, :].rearrange("p a b -> p (a b)"), pair[0][:, :],
                          ACT.Copy).then_inc(kd_hi_ok.sem, 1)
                    elif kind in ("zA", "zB"):
                        act.wait_ge(scratch_free.sem, scratch_free.at(i, scratch_no(u) - 2))
                        A(pair[0][:, :], bank[:, :], ACT.Tanh, scale=0.5).then_inc(z_tanh_ok.sem, 1)
                    elif kind in ("mA", "mB"):
                        m = M_UNITS.index(u)
                        if m >= 12:
                            act.wait_ge(y_sum_ok.sem, y_sum_ok.at(i, m - 11))
                        elif m >= 4:
                            act.wait_ge(freed_dve.sem, freed_dve.at(i, dve_no(M_UNITS[m - 4] + 2)))
                        A(gate[m % 4][:, :], bank[:, :], ACT.Tanh, scale=0.5,
                          bias=half_bm[:, m:m + 1]).then_inc(freed_act.sem, 1)
                    elif kind == "yB":
                        e = YB_UNITS.index(u)
                        act.wait_ge(y_sum_ok.sem, y_sum_ok.at(i, e + 1))
                        A(y_hi[:, e, :], y_sum[:, e, :], ACT.Copy).then_inc(y_hi_ok.sem, 1)
                    elif kind == "out":
                        if u == OUT_UNITS[0]:
                            act.wait_ge(y_lo_ok.sem, y_lo_ok.at(i, KD))
                        A(rows[:, 2 * j:2 * j + 2, idx * CW:(idx + 1) * CW],
                          bank[:, :].rearrange("p (a b) -> p a b", a=2), ACT.Copy) \
                            .then_inc(freed_act.sem, 1)
                for half in range(2):
                    split_w(i, NC + 1, half)
            assert seq["n"] == act_seq.per, seq

        @block.vector
        def _(dve):
            for c in DVE_COUNTS:
                c.credit(dve)
            V = nc.vector
            seq = {"n": 0}

            def link(i, ins):
                seq["n"] += 1
                ins.then_inc(dve_seq.sem, 1)
                dve.wait_ge(dve_seq.sem, dve_seq.at(i, seq["n"]))

            def row_stats(i, stat, src, t, half):
                link(i, V.bn_stats(stat[:, t, half, :], src[:, t, half * 512:(half + 1) * 512]))

            def row_mean(i, stat, sm):
                v = stat[:, :, :, :].rearrange("p t h (e c) -> p (t h e) c", c=3)
                flat = sm[:, :, :].rearrange("p a b -> p (a b)")
                link(i, V.tensor_tensor(flat[:, 0:16], v[:, :, 1], v[:, :, 1], ALU.mult))
                link(i, V.scalar_tensor_tensor(flat[:, 16:32], flat[:, 0:16], float(P * 2), v[:, :, 2],
                                               ALU.mult, ALU.add))
                link(i, V.reduce_sum(sm[:, 8, :], flat[:, 16:32].rearrange("p (t e) -> p t e", t=NT),
                                     AX.X))
                link(i, V.tensor_scalar(sm[:, 9, :], sm[:, 8, :], 1.0 / D, EPS, ALU.mult, ALU.add))

            def row_rstd(i, sm):
                bits = sm[:, :, :].bitcast(i32)
                link(i, V.tensor_scalar(bits[:, 0, :], bits[:, 9, :], 1, None, ALU.arith_shift_right))
                link(i, V.tensor_scalar(bits[:, 5, :], bits[:, 0, :], -1, 0x5F3759DF, ALU.mult, ALU.add))
                for _ in range(NEWTON):
                    link(i, V.scalar_tensor_tensor(sm[:, 2, :], sm[:, 5, :], -0.5, sm[:, 9, :],
                                                   ALU.mult, ALU.mult))
                    link(i, V.tensor_tensor(sm[:, 3, :], sm[:, 2, :], sm[:, 5, :], ALU.mult))
                    link(i, V.scalar_tensor_tensor(sm[:, 5, :], sm[:, 3, :], 1.5, sm[:, 5, :],
                                                   ALU.add, ALU.mult))

            def x_norm(i, t):
                V.tensor_scalar(x_in[:, t, :], x_in[:, t, :], x_sm[:, 5, t:t + 1], None, ALU.mult) \
                    .then_inc(x_norm_ok.sem, 1)

            def x_split(i, k):
                dve.wait_ge(h_hi_ok.sem, h_hi_ok.at(i, k + 1))
                V.scalar_tensor_tensor(h_lo[:, k, :], pm[k % 4][:, :], cols_sb[:, k:k + 1],
                                       as_f32(h_hi[:, k, :]), ALU.mult, ALU.subtract) \
                    .then_inc(h_lo_ok.sem, 1)

            seq["n"] = dve_seq.per - dve_seq.done_before
            dve.wait_ge(const_in, 48)
            dve.wait_ge(x_in_ok.sem, x_in_ok.at(-1, NT))
            for t in range(NT):
                for half in range(2):
                    row_stats(-1, x_stat, x_in, t, half)
            row_mean(-1, x_stat, x_sm)
            row_rstd(-1, x_sm)
            for t in range(NT):
                x_norm(-1, t)
            for k in range(KD):
                x_split(-1, k)
            seq["n"] += 1
            assert seq["n"] == dve_seq.per, seq
            V.tensor_scalar(half_bm[:, :], cols_sb[:, 16:32], 0.5, None, ALU.mult) \
                .then_inc(dve_seq.sem, 1)

            prep = {"n": 0}
            dve.wait_ge(stored.sem, stored.at(-1, NT))

            def step(ins):
                prep["n"] += 1
                ins.then_inc(prep_ok, 1)
                dve.wait_ge(prep_ok, prep["n"])

            a3 = ang[:, :].rearrange("p (t f) -> p t f", t=NB * NT)
            step(V.tensor_copy(pos_f[:, :], pos_i[:, :]))
            step(V.tensor_tensor(a3, pos_f[:, :].unsqueeze(2).broadcast_to([P, NB * NT, HD // 2]),
                                 cs["inv_freq"].unsqueeze(1).broadcast_to([P, NB * NT, HD // 2]), ALU.mult))
            magic = float(1.5 * 2 ** 23)
            for scale, parts in ((4096.0, 6), (1.0, 6)):
                step(V.tensor_scalar(turns[:, :], ang[:, :], float(1 / (2 * np.pi * scale)), magic,
                                     ALU.mult, ALU.add))
                step(V.tensor_scalar(turns[:, :], turns[:, :], -magic, scale, ALU.add, ALU.mult))
                for part in two_pi_parts(parts):
                    step(V.scalar_tensor_tensor(ang[:, :], turns[:, :], -part, ang[:, :],
                                                ALU.mult, ALU.add))
            step(V.tensor_scalar(ang[:, :], ang[:, :], 3.1415925, -3.1415925, ALU.min, ALU.max))
            step(V.scalar_tensor_tensor(r_abs[:, :], ang[:, :], -1.0, ang[:, :], ALU.mult, ALU.max))
            assert prep["n"] == ROPE_PREP
            dve.wait_ge(trig_ok, 2)
            dve.wait_ge(zeroed, 3)

            def rope(i, u):
                kind, idx, j = UNIT_AT[u]
                heads = 2 if kind == "kvB" else CW // HD
                r_cos, r_sin = scratch[SCRATCH_USERS.index(u) % 2]
                for a in range(2):
                    o = pu[u % NPB][:, a * CW:a * CW + heads * HD].rearrange("p (h e) -> p h e", e=HD // 2)
                    oh = pu[u % NPB][:, a * CW:a * CW + heads * HD] \
                        .rearrange("p (h x e) -> p h x e", x=2, e=HD // 2)
                    dst = slice(a * CW, a * CW + heads * HD)
                    table = ds(i * NT + (2 * j + a), 1)
                    V.tensor_tensor(r_cos[:, dst].rearrange("p (h e) -> p h e", e=HD // 2), o,
                                    cos[:, table, :].broadcast_to([P, 2 * heads, HD // 2]), ALU.mult)
                    d = r_sin[:, dst].rearrange("p (h x e) -> p h x e", x=2, e=HD // 2)
                    for x_ in range(2):
                        last = V.tensor_tensor(d[:, :, x_, :], oh[:, :, 1 - x_, :],
                                               sin[:, table, :].broadcast_to([P, heads, HD // 2]), ALU.mult)
                return last

            with dve.Fori(0, NB) as i:
                seq["n"] = 0
                for u in range(SLOTS):
                    if u in LOGITS:
                        t = LOGITS[u]
                        dve.wait_ge(softplus_ok.sem, softplus_ok.at(i, t + 1))
                        if t >= 2:
                            dve.wait_ge(suffix_ok.sem, suffix_ok.at(i, t - 1))
                        V.scalar_tensor_tensor(log_a[t % 2][:, :], pm[0][:, :], 0.0, soft[:, :],
                                               ALU.min, ALU.subtract).then_inc(log_a_ok.sem, 1)
                    if u in UPD:
                        n = UPD[u]
                        h, t = divmod(n, NT)
                        dve.wait_ge(upd_ok.sem, upd_ok.at(i, n + 1))
                        if n == 0:
                            dve.wait_ge(decay_ok.sem, decay_ok.at(i, NT + 1))
                        dve.wait_ge(s_lo_ok.sem, s_lo_ok.at(i, 2 * n))
                        V.scalar_tensor_tensor(s_mid[:, :], state[:, h, :], decay_s[:, t, h, 0:1],
                                               pm[0][:, 0:DV], ALU.mult, ALU.add).then_inc(state_ok.sem, 1)
                        dve.wait_ge(state_ok.sem, state_ok.at(i, 2 * n + 1))
                        V.scalar_tensor_tensor(state[:, h, :], s_mid[:, :], decay_s[:, t, h, 1:2],
                                               pm[1][:, 0:DV], ALU.mult, ALU.add).then_inc(state_ok.sem, 1)
                    if u in NORM:
                        h = NORM[u]
                        dve.wait_ge(ssq_ok.sem, ssq_ok.at(i, h + 1))
                        V.tensor_scalar(mean_a[:, :], pm[4][:, :], 1.0 / DV, EPS, ALU.mult, ALU.add) \
                            .then_inc(mean_a_ok.sem, 1)
                        sq = square[0]
                        dve.wait_ge(rstd_a0_ok.sem, rstd_a0_ok.at(i, h + 1))
                        link(i, V.scalar_tensor_tensor(sq[:, :], rstd_a[:, :], -0.5, mean_a[:, :],
                                                       ALU.mult, ALU.mult))
                        link(i, V.tensor_tensor(sq[:, :], sq[:, :], rstd_a[:, :], ALU.mult))
                        link(i, V.scalar_tensor_tensor(rstd_a[:, :], sq[:, :], 1.5, rstd_a[:, :],
                                                       ALU.add, ALU.mult))
                        for j in range(2):
                            e = 2 * h + j
                            V.scalar_tensor_tensor(oa[:, e, :], oa[:, e, :], cols_sb[:, 8 + e:9 + e],
                                                   rstd_a[:, :], ALU.mult, ALU.mult) \
                                .then_inc(oa_norm_ok.sem, 1)
                    if u == KTR:
                        V.tensor_copy(k_even[:, :, 0, CH:P], k_odd[:, :, NT - 1, CH:P]) \
                            .then_inc(k_even_ok.sem, 1)
                        dve.wait_ge(k_odd_ok.sem, k_odd_ok.at(i, 2))
                        V.tensor_copy(k_even[:, :, :, 0:CH], k_odd[:, :, :, 0:CH]).then_inc(k_even_ok.sem, 1)
                        V.tensor_copy(k_even[:, :, 1:NT, CH:P], k_odd[:, :, 0:NT - 1, CH:P]) \
                            .then_inc(k_even_ok.sem, 1)
                    if u in PTR:
                        s = PTR[u]
                        dve.wait_ge(ptr_ok.sem, ptr_ok.at(i, s + 1))
                        dve.wait_ge(pv_ok.sem, pv_ok.at(i, s))
                        V.tensor_copy(prob_t[:, 4:8, :].rearrange("p a b -> p (a b)"), pm[2][:, :]) \
                            .then_inc(pt_odd_ok.sem, 1)
                    if u in SCORE:
                        s = SCORE[u]
                        g = s // NT
                        tp, se = top[s % 2], sink_e[s % 2]
                        dve.wait_ge(score_ok.sem, score_ok.at(i, s + 1))
                        for par in range(2):
                            ins = V.reduce_max(tp[:, 4 * par:4 * par + 4],
                                               pm[1 + par][:, :].rearrange("p (e k) -> p e k", e=4), AX.X)
                            link(i, ins)
                        link(i, V.scalar_tensor_tensor(tp[:, :], tp[:, :], HD ** -0.5,
                                                       sink_sb[:, 8 * g:8 * g + 8], ALU.mult, ALU.max))
                        if s >= 2:
                            dve.wait_ge(ptr_ok.sem, ptr_ok.at(i, s - 1))
                        for par in range(2):
                            ins = V.scalar_tensor_tensor(
                                prob[s % 2][:, 4 * par:4 * par + 4, :],
                                pm[1 + par][:, :].rearrange("p (e k) -> p e k", e=4), HD ** -0.5,
                                tp[:, 4 * par:4 * par + 4].unsqueeze(2).broadcast_to([P, 4, P]),
                                ALU.mult, ALU.subtract)
                        ins.then_inc(shift_ok.sem, 1)
                        V.tensor_tensor(se[:, :], sink_sb[:, 8 * g:8 * g + 8], tp[:, :], ALU.subtract) \
                            .then_inc(sink_d_ok.sem, 1)
                        if s == NT:
                            V.memset(mask_sb[:, :], 0.0)
                    if u - 1 in SCORE:
                        s = SCORE[u - 1]
                        dve.wait_ge(p_exp_ok.sem, p_exp_ok.at(i, 2 * s + 2))
                        link(i, V.reduce_sum(den[s % 2][:, :], prob[s % 2][:, :, :], AX.X))
                        V.tensor_tensor(den[s % 2][:, :], den[s % 2][:, :], sink_e[s % 2][:, :], ALU.add) \
                            .then_inc(den0_ok.sem, 1)
                        dve.wait_ge(den0_ok.sem, den0_ok.at(i, s + 1))
                        V.reciprocal(den[s % 2][:, :], den[s % 2][:, :]).then_inc(den_ok.sem, 1)
                    if u in XSTAT:
                        if XSTAT[u] == 0:
                            dve.wait_ge(x_in_ok.sem, x_in_ok.at(i, NT))
                        for half in range(2):
                            row_stats(i, x_stat, x_in, XSTAT[u], half)
                    if u == XRSTD:
                        row_mean(i, x_stat, x_sm)
                        row_rstd(i, x_sm)
                    if u in XNORM:
                        x_norm(i, XNORM[u])
                    if u in XTR:
                        for k in XTR[u]:
                            x_split(i, k)
                    if u - 1 in Z_UNITS:
                        kind, idx, j = UNIT_AT[u - 1]
                        e = 2 * idx + j
                        pair = scratch[SCRATCH_USERS.index(u - 1) % 2]
                        dve.wait_ge(freed_dve.sem, freed_dve.at(i, dve_no(u - 1)))
                        if kind == "zA":
                            src = oa
                            dve.wait_ge(oa_norm_ok.sem, oa_norm_ok.at(i, e + 1))
                        else:
                            src = ob
                            dve.wait_ge(ob_ok.sem, ob_ok.at(i, 4 * (e // 4) + 4))
                        V.scalar_tensor_tensor(pair[0][:, :], src[:, e, :], 0.25, pair[0][:, :],
                                               ALU.mult, ALU.mult) \
                            .then_inc(gated_ok.sem, 1)
                    if u not in UNIT_AT:
                        continue
                    kind, idx, j = UNIT_AT[u]
                    bank = pu[u % NPB]
                    if u in SCRATCH_USERS:
                        pair = scratch[SCRATCH_USERS.index(u) % 2]
                    free = freed_dve.sem
                    if kind == "vA":
                        dve.wait_ge(v_hi_ok.sem, v_hi_ok.at(i, V_UNITS.index(u) + 1))
                        hi = v_hi[idx % 2][:, 2 * j:2 * j + 2, :].rearrange("p a b -> p (a b)")
                        V.tensor_tensor(v_lo[idx % 2][:, 2 * j:2 * j + 2, :].rearrange("p a b -> p (a b)"),
                                        bank[:, :], as_f32(hi), ALU.subtract).then_inc(free, 1)
                    elif kind == "qA":
                        dve.wait_ge(q_hi_ok.sem, q_hi_ok.at(i, Q_UNITS.index(u) + 1))
                        V.scalar_tensor_tensor(q_lo[idx][:, j, :], bank[:, :], DK ** -0.5,
                                               as_f32(q_hi[idx][:, j, :]), ALU.mult, ALU.subtract) \
                            .then_inc(free, 1)
                    elif kind == "kA":
                        dve.wait_ge(unit_done.sem, unit_done.at(i, unit_no(u)))
                        dve.wait_ge(decay_ok.sem, decay_ok.at(i, 2 * j + 2))
                        dve.wait_ge(scratch_free.sem, scratch_free.at(i, scratch_no(u) - 2))
                        V.tensor_tensor(pair[0][:, :].rearrange("p (a b) -> p a b", a=2),
                                        bank[:, :].rearrange("p (a b) -> p a b", a=2),
                                        decay_w[:, 2 * j:2 * j + 2, idx * CW:(idx + 1) * CW], ALU.mult) \
                            .then_inc(free, 1)
                    elif kind in ("zA", "zB"):
                        dve.wait_ge(z_tanh_ok.sem, z_tanh_ok.at(i, Z_UNITS.index(u) + 1))
                        V.scalar_tensor_tensor(pair[0][:, :], pair[0][:, :], 1.0, bank[:, :],
                                               ALU.add, ALU.mult).then_inc(free, 1)
                    elif kind == "yA":
                        e = 2 * idx + j
                        dve.wait_ge(freed_act.sem, freed_act.at(i, act_no(u - 2)))
                        dve.wait_ge(unit_done.sem, unit_done.at(i, unit_no(u)))
                        V.scalar_tensor_tensor(y_sum[:, e, :], gate[e % 4][:, :], 1.0, bank[:, :],
                                               ALU.add, ALU.mult).then_inc(free, 1)
                    elif kind == "yB":
                        e = 2 * idx + j
                        gt = gate[e % 4]
                        dve.wait_ge(freed_act.sem, freed_act.at(i, act_no(u - 2)))
                        dve.wait_ge(unit_done.sem, unit_done.at(i, unit_no(u)))
                        V.scalar_tensor_tensor(gt[:, :], gt[:, :], 1.0, bank[:, :],
                                               ALU.add, ALU.mult).then_inc(free, 1)
                        dve.wait_ge(freed_dve.sem, freed_dve.at(i, dve_no(u)))
                        V.tensor_tensor(y_sum[:, e, :], y_sum[:, e, :], gt[:, :], ALU.add) \
                            .then_inc(y_sum_ok.sem, 1)
                    elif kind in ("kvB", "qB"):
                        dve.wait_ge(unit_done.sem, unit_done.at(i, unit_no(u)))
                        dve.wait_ge(scratch_free.sem, scratch_free.at(i, scratch_no(u) - 2))
                        last = rope(i, u)
                        if kind == "kvB":
                            if j == 0:
                                link(i, V.tensor_copy(v_even[CH:P, 0, :], v_odd[CH:P, NT - 1, :]))
                            last = V.tensor_copy(v_odd[:, 2 * j:2 * j + 2, :],
                                                 bank[:, :].rearrange("p (a b) -> p a b", a=2)[:, :, P:2 * P])
                        last.then_inc(free, 1)
                        if kind == "kvB" and j == 1:
                            dve.wait_ge(freed_dve.sem, freed_dve.at(i, dve_no(u)))
                            link(i, V.tensor_copy(v_even[0:CH, :, :], v_odd[0:CH, :, :]))
                            V.tensor_copy(v_even[CH:P, 1:NT, :], v_odd[CH:P, 0:NT - 1, :]) \
                                .then_inc(v_even_ok.sem, 1)
                    elif kind == "out":
                        if idx % 2:
                            dve.wait_ge(freed_act.sem, freed_act.at(i, act_no(u)))
                            for t in (2 * j, 2 * j + 1):
                                row_stats(i, o_stat, rows, t, idx // 2)
                row_mean(i, o_stat, o_sm)
                row_rstd(i, o_sm)
                for n, t in enumerate((2, 3, 0, 1)):
                    V.scalar_tensor_tensor(rows[:, t, :], rows[:, t, :], o_sm[:, 5, t:t + 1], gpost_sb[:, :],
                                           ALU.mult, ALU.mult).then_inc(o_scaled_ok.sem, 1)
                dve.wait_ge(x_res_ok.sem, x_res_ok.at(i, NT))
                for n, t in enumerate((0, 1)):
                    dve.wait_ge(o_scaled_ok.sem, o_scaled_ok.at(i, 3 + n))
                    V.tensor_tensor(rows[:, t, :], rows[:, t, :], x_res[:, t, :], ALU.add) \
                        .then_inc(o_dve_ok.sem, 1)
            assert seq["n"] == dve_seq.per, seq

        @block.gpsimd
        def _(pool):
            for c in POOL_COUNTS:
                c.credit(pool)
            G = nc.gpsimd
            TT = G.tensor_tensor

            def split_w(i, c, half):
                pool.wait_ge(w_hi_ok.sem, w_hi_ok.at(i, w_half_no(c, half)))
                ks = slice(half * (KD // 2), (half + 1) * (KD // 2))
                TT(w_lo[c % 2][:, ks, :], w_raw[half][:, :, :], as_f32(w_hi[c % 2][:, ks, :]),
                   ALU.subtract).then_inc(w_lo_ok.sem, 1)

            for dst, src in ((wdecay_sb, w_decay), (pos_i, pos), (sink_sb, sinks), (gpost_sb, gpost)):
                pool.dma_start(dst[:, :], src).then_inc(stored.sem, 16)
            G.memset(state[:, :, :], 0.0).then_inc(zeroed, 1)
            G.memset(k_odd[:, :, :, :], 0.0).then_inc(zeroed, 1)
            G.memset(v_odd[:, :, :], 0.0).then_inc(zeroed, 1)
            for c in (NC, NC + 1):
                for half in range(2):
                    split_w(-1, c, half)

            with pool.Fori(0, NB) as i:
                for u in range(SLOTS):
                    if u >= 2:
                        split_w(i, u // 2 + 1, u % 2)
                    if u in UPD:
                        n = UPD[u]
                        pool.wait_ge(read_ok.sem, read_ok.at(i, n))
                        for c in range(2):
                            pool.wait_ge(s_hi_ok.sem, s_hi_ok.at(i, 2 * n + c + 1))
                            src = s_mid[:, :] if c == 0 else state[:, n // NT, :]
                            TT(s_lo[:, c, :], src, as_f32(s_hi[:, c, :]), ALU.subtract) \
                                .then_inc(s_lo_ok.sem, 1)
                    if u - 1 in SCORE:
                        s = SCORE[u - 1]
                        pool.wait_ge(den_ok.sem, den_ok.at(i, s + 1))
                        pr = prob[s % 2]
                        TT(pr[:, :, :], pr[:, :, :], den[s % 2][:, :].unsqueeze(2).broadcast_to([P, GH, P]),
                           ALU.mult).then_inc(p_norm_ok.sem, 1)
                    if u - 1 in Z_UNITS:
                        _, idx, j = UNIT_AT[u - 1]
                        e = 2 * idx + j
                        pool.wait_ge(g_hi_ok.sem, g_hi_ok.at(i, Z_UNITS.index(u - 1) + 1))
                        TT(g_lo[:, e, :], scratch[SCRATCH_USERS.index(u - 1) % 2][0][:, :],
                           as_f32(g_hi[:, e, :]), ALU.subtract).then_inc(scratch_free.sem, 1)
                    if u not in UNIT_AT:
                        continue
                    kind, idx, j = UNIT_AT[u]
                    if u in SCRATCH_USERS:
                        pair = scratch[SCRATCH_USERS.index(u) % 2]
                    done = scratch_free.sem
                    if kind == "kA":
                        pool.wait_ge(kd_hi_ok.sem, kd_hi_ok.at(i, K_UNITS.index(u) + 1))
                        rows_ = slice(2 * j, 2 * j + 2)
                        TT(kd_lo[:, rows_, :].rearrange("p a b -> p (a b)"), pair[0][:, :],
                           as_f32(kd_hi[:, rows_, :].rearrange("p a b -> p (a b)")), ALU.subtract) \
                            .then_inc(done, 1)
                    elif kind in ("kvB", "qB"):
                        pool.wait_ge(freed_dve.sem, freed_dve.at(i, dve_no(u)))
                        r_cos, r_sin = pair
                        if kind == "qB":
                            dst = q_rope[:, 2 * j:2 * j + 2, idx * CW:(idx + 1) * CW] \
                                .rearrange("p t (h x e) -> p t h x e", x=2, e=HD // 2)
                            c4, s4 = (r[:, :].rearrange("p (t h x e) -> p t h x e", t=2, x=2, e=HD // 2)
                                      for r in (r_cos, r_sin))
                            for x_, op in enumerate((ALU.subtract, ALU.add)):
                                ins = TT(dst[:, :, :, x_, :], c4[:, :, :, x_, :], s4[:, :, :, x_, :], op)
                        else:
                            for a in range(2):
                                c4, s4 = (r[:, a * CW:a * CW + 2 * HD]
                                          .rearrange("p (h x e) -> p h x e", x=2, e=HD // 2)
                                          for r in (r_cos, r_sin))
                                for copy in range(2):
                                    dst = k_rope[:, 2 * j + a, :, copy, :] \
                                        .rearrange("p h (x e) -> p h x e", x=2)
                                    for x_, op in enumerate((ALU.subtract, ALU.add)):
                                        ins = TT(dst[:, :, x_, :], c4[:, :, x_, :], s4[:, :, x_, :], op)
                        ins.then_inc(done, 1)
                    elif kind == "yB":
                        e = 2 * idx + j
                        pool.wait_ge(y_hi_ok.sem, y_hi_ok.at(i, e + 1))
                        TT(y_lo[:, e, :], y_sum[:, e, :], as_f32(y_hi[:, e, :]), ALU.subtract) \
                            .then_inc(y_lo_ok.sem, 1)
                for half in range(2):
                    split_w(i, NC + 1, half)
                pool.wait_ge(x_res_ok.sem, x_res_ok.at(i, NT))
                for n, t in enumerate((2, 3)):
                    pool.wait_ge(o_scaled_ok.sem, o_scaled_ok.at(i, n + 1))
                    TT(rows[:, t, :], rows[:, t, :], x_res[:, t, :], ALU.add).then_inc(o_pool_ok.sem, 1)
                for t in range(NT):
                    src = o_dve_ok if t < 2 else o_pool_ok
                    pool.wait_ge(src.sem, src.at(i, t % 2 + 1))
                    pool.dma_start(out[ds(i * TB + t * P, P), :], rows[:, t, :]).then_inc(stored.sem, 16)


ROPE_PREP = 2 + 2 * (2 + 6) + 2


INS = ["x", "w", "w_decay", "pos", "cols", "sinks", "gpost", "consts", "mask"]


def kernel(x, positions, g_pre, w_in, w_decay_up, b_decay_up, g_gla, attn_sinks,
           w_branch_gla, w_branch_swa, b_merge, w_out, g_post):
    import concourse.bacc as bacc
    from concourse.bass_utils import run_bass_kernel_spmd as run

    w_in, wa, wb, wo = (np.asarray(a)[0] for a in (w_in, w_branch_gla, w_branch_swa, w_out))
    first = dict(qA=0, kA=512, vA=1024, lr=2048, zA=2064, qB=3088, kvB=4112, zB=4368, mA=5392, mB=6416)
    w = np.zeros((NC, P, KD, CW), np.float32)
    for c, (kind, idx) in enumerate(CHUNKS):
        src, col = {"yA": (wa, 0), "yB": (wb, 0), "out": (wo, 0)}.get(kind, (w_in, first.get(kind)))
        width = RANK if kind == "lr" else CW
        part = src[:, col + idx * CW:col + idx * CW + width]
        w[c, :, :, :width] = part.reshape(KD, P, width).transpose(1, 0, 2)
    w_decay = np.zeros((32, HEADS_A * DK), np.float32)
    w_decay[:RANK] = np.asarray(w_decay_up)[0]
    w_decay[RANK] = np.asarray(b_decay_up)[0]
    cols = np.concatenate([np.asarray(a)[0].reshape(-1, P).T for a in (g_pre, g_gla, b_merge)], axis=1)
    sinks = np.asarray(attn_sinks)[0].reshape(2, 4, 2).transpose(0, 2, 1).reshape(1, 16)
    arrays = {
        "x": np.ascontiguousarray(np.asarray(x)[0]), "w": w, "w_decay": w_decay,
        "pos": np.ascontiguousarray(np.asarray(positions)[0].reshape(NB * NT, P).T),
        "cols": np.ascontiguousarray(cols), "sinks": np.ascontiguousarray(np.broadcast_to(sinks, (P, 16))),
        "gpost": np.ascontiguousarray(np.broadcast_to(np.asarray(g_post)[0], (P, D))),
        "consts": const_array(), "mask": mask_array(),
    }
    nc = bacc.Bacc("TRN2", target_bir_lowering=False, num_devices=1, dynamic_dma_scratch_size=768)
    args = [nc.dram_tensor(f"in_{n}", arrays[n].shape, mybir.dt.from_np(arrays[n].dtype),
                           kind="ExternalInput").ap() for n in INS]
    out = nc.dram_tensor("out_y", (SEQ, D), mybir.dt.float32, kind="ExternalOutput").ap()
    build(nc, *args, out)
    r = run(nc, [{f"in_{n}": arrays[n] for n in INS}], core_ids=[0])
    return r.results[0]["out_y"].reshape(1, SEQ, D)
```

```python
import numpy as np
import concourse.bass as bass
from concourse import mybir
from contextlib import ExitStack

P = 128
D = 1024
SEQ = 2048
TB = 512
NB = SEQ // TB
NT = TB // P
KD = D // P
CW = 256
HEADS_A, DK, DV = 4, 128, 256
CH = 64
HD = 64
GH = 8
RANK = 16
TAU = 16.0
EPS = 1e-6
NEG = -1e30

CHUNKS = ([("lr", 0), ("qA", 0), ("vA", 0), ("kA", 0), ("vA", 1), ("qA", 1), ("vA", 2), ("kA", 1),
           ("vA", 3), ("zA", 0), ("zA", 1), ("zA", 2), ("kvB", 0), ("qB", 0), ("qB", 1), ("zA", 3),
           ("qB", 2), ("qB", 3)]
          + [c for j in range(4) for c in (("mA", j), ("yA", j))]
          + [("zB", j) for j in range(4)]
          + [c for j in range(4) for c in (("mB", j), ("yB", j))]
          + [("out", j) for j in range(4)])
NC = len(CHUNKS)
TOKEN_MAJOR = ("kA", "vA", "kvB", "qB", "out")
UNITS = [(2 * c + j, kind, idx, j) for c, (kind, idx) in enumerate(CHUNKS) for j in range(2)
         if not (kind == "lr" and j)]
NU = len(UNITS)
SLOTS = 2 * NC
UNIT_AT = {u: (kind, idx, j) for u, kind, idx, j in UNITS}
FREED_BY_ACT = [u for u, kind, _, _ in UNITS if kind in ("lr", "qA", "mA", "mB", "out")]
FREED_BY_DVE = [u for u, kind, _, _ in UNITS if kind not in ("lr", "qA", "mA", "mB", "out")]
SCRATCH_USERS = [u for u, kind, _, _ in UNITS if kind in ("kA", "zA", "zB", "kvB", "qB")]
NEWTON = 3
NPB = 3

DVE_HALVES = [(2, 0), (2, 1), (13, 1), (NC + 1, 1)]
POOL_HALVES = [(c, half) for c in range(2, NC + 2) for half in range(2) if (c, half) not in DVE_HALVES]

UNIT_LIST = [u for u, _, _, _ in UNITS]


def unit_no(u):
    return UNIT_LIST.index(u) + 1


def dve_no(u):
    return FREED_BY_DVE.index(u) + 1


def act_no(u):
    return FREED_BY_ACT.index(u) + 1


def scratch_no(u):
    return SCRATCH_USERS.index(u) + 1


def of_kind(*kinds):
    return [u for u, kind, _, _ in UNITS if kind in kinds]


Z_UNITS = of_kind("zA", "zB")
V_UNITS, Q_UNITS, K_UNITS = of_kind("vA"), of_kind("qA"), of_kind("kA")
M_UNITS, YB_UNITS = of_kind("mA", "mB"), of_kind("yB")
ROPE_UNITS = of_kind("kvB", "qB")
OUT_UNITS = of_kind("out")

LOGITS = {3: (0, 1), 5: (2, 3)}
LOGIT_BANK = [0, 3, 4, 0]
SUFFIX = {5: (0, 1), 7: (2, 3)}
SUFFIX_BANK = [1, 3, 1, 3]
UPD = {8 + n: n for n in range(16)}
READ = {9 + n: n for n in range(16)}
OTR = {u: e for e, u in enumerate(of_kind("zA"))}
OTR_BANK = [3, 4, 3, 4, 3, 4, 2, 3]
KTR = 28
QTR = {32 + 3 * s: s for s in range(8)}
SCORE = {33 + 3 * s: s for s in range(8)}
PTR = {35 + 3 * s: s for s in range(8)}
PV = {36 + 3 * s: s for s in range(8)}
Y_SPLIT = {u + 1: (e,) for e, u in enumerate(YB_UNITS[:-1])}
Y_SPLIT[YB_UNITS[-1]] = (KD - 2, KD - 1)
XSTAT = {66 + t: t for t in range(NT)}
XRSTD = 70
XNORM = {71 + t: t for t in range(NT)}
XTR = {76 + g: (2 * g, 2 * g + 1) for g in range(4)}



def two_pi_parts(n):
    rest, parts = 2 * np.pi, []
    for _ in range(n - 1):
        unit = 2.0 ** (np.floor(np.log2(abs(rest))) - 6)
        part = float(np.round(rest / unit) * unit)
        parts.append(part)
        rest -= part
    return parts + [float(np.float32(rest))]


CONST_COLS = dict(ident=128, later=128, chunk_of=2, bias_row=1, one=1,
                  half_pi=1, inv_freq=32)


def const_array():
    c = {k: np.zeros((P, n), np.float32) for k, n in CONST_COLS.items()}
    r = np.arange(P)
    c["ident"][r, r] = 1
    c["later"][:] = (r[:, None] > r[None, :]) & (r[:, None] // CH == r[None, :] // CH)
    c["chunk_of"][r, r // CH] = 1
    c["bias_row"][2 * RANK] = 1
    c["one"][:] = 1
    c["half_pi"][:] = np.pi / 2
    c["inv_freq"][:] = (10000.0 ** (-np.arange(HD // 2) / (HD // 2))).astype(np.float32)
    return np.concatenate(list(c.values()), axis=1)


class Count:

    def __init__(self, sem, per_block, unit=1, done_before=0):
        self.sem, self.per, self.unit, self.done_before = sem, per_block, unit, done_before

    def credit(self, eng):
        if self.per > self.done_before:
            eng.sem_inc(self.sem, (self.per - self.done_before) * self.unit)

    def at(self, i, n):
        return i * (self.per * self.unit) + (self.per + n) * self.unit


def build(nc, x, w, w_decay, pos, cols, sinks, gpost, consts, out):
    f32, f32r, i32 = mybir.dt.float32, mybir.dt.float32r, mybir.dt.int32
    ALU, ACT, AX = mybir.AluOpType, mybir.ActivationFunctionType, mybir.AxisListType
    ds = bass.ds

    with ExitStack() as ctx:
        place = {"at": (nc.sbuf_base + 31) // 32 * 32}

        def region(nbytes):
            at = place["at"]
            place["at"] = at + nbytes
            return at

        def tile(name, shape, dt=f32, at=None):
            nbytes = 4 * int(np.prod(shape[1:]))
            return nc.alloc_sbuf_tensor_at(name, list(shape), dt,
                                           offset=region((nbytes + 31) // 32 * 32) if at is None else at)

        h_hi = tile("h_hi", [P, KD, TB], f32r)
        h_lo = tile("h_lo", [P, KD, TB], f32r)
        w_raw = [tile(f"w_raw{s}", [P, KD // 2, CW]) for s in range(2)]
        w_hi = [tile(f"w_hi{s}", [P, KD, CW], f32r) for s in range(2)]
        w_lo = [tile(f"w_lo{s}", [P, KD, CW], f32r) for s in range(2)]
        at = region(2 * KD * TB * 4)
        g_hi = tile("g_hi", [P, KD, TB], f32r, at)
        g_lo = tile("g_lo", [P, KD, TB], f32r, at + KD * TB * 4)
        x_res = tile("x_res", [P, NT, D], f32, at)
        K1 = 1024
        at = region(40 * K1)
        v_hi = [tile(f"v_hi{s}", [P, NT, DV], f32r, at + 4 * K1 * s) for s in range(2)]
        v_lo = [tile(f"v_lo{s}", [P, NT, DV], f32r, at + (8 + 4 * s) * K1) for s in range(2)]
        q_a = [tile(f"q_a{s}", [P, 2, TB], f32, at + (16 + 4 * s) * K1) for s in range(2)]
        la_hi = [tile(f"la_hi{s}", [P, TB], f32r, at + (24 + 2 * s) * K1) for s in range(2)]
        la_lo = [tile(f"la_lo{s}", [P, TB], f32r, at + (28 + 2 * s) * K1) for s in range(2)]
        kd_hi = tile("kd_hi", [P, NT, 2 * DK], f32r, at + 32 * K1)
        kd_lo = tile("kd_lo", [P, NT, 2 * DK], f32r, at + 36 * K1)
        q_rope = tile("q_rope", [P, NT, D], f32, at)
        ob = tile("ob", [P, KD, TB], f32, at + 16 * K1)
        y_hi = tile("y_hi", [P, KD, TB], f32r, at)
        y_lo = tile("y_lo", [P, KD, TB], f32r, at + 16 * K1)
        at = region(KD * TB * 4)
        oa = tile("oa", [P, NT, D], f32, at)
        y_sum = tile("y_sum", [P, KD, TB], f32, at)
        rows = tile("rows", [P, NT, D], f32, at)
        at = region(16 * K1)
        decay_w = tile("decay_w", [P, NT, HEADS_A * DK], f32, at)
        s_mid = tile("s_mid", [P, DV], f32, at + 12 * K1)
        soft1 = tile("soft1", [P, TB], f32, at + 14 * K1)
        k_rope = tile("k_rope", [P, NT, 2, 2, HD], f32, at)
        prob = [tile(f"prob{s}", [P, GH, P], f32, at + 4 * K1 * s) for s in range(2)]
        prob_t = tile("prob_t", [P, GH, P], f32, at + 8 * K1)
        q_t = [tile(f"q_t{s}", [P, NT, P], f32, at + (12 + 2 * s) * K1) for s in range(2)]
        x_in = tile("x_in", [P, NT, D], f32, at)
        at = region(8 * K1)
        gate = [tile(f"gate{s}", [P, TB], f32, at + 2 * K1 * s) for s in range(4)]
        soft = [tile("soft0", [P, TB], f32, at), soft1]
        log_a = [tile(f"log_a{s}", [P, TB], f32, at + (2 + 2 * s) * K1) for s in range(2)]
        lr_t = tile("lr_t", [P, TB], f32, at + 6 * K1)
        at = region(8 * K1)
        scratch = [[tile(f"scratch{s}{j}", [P, TB], f32, at + (4 * s + 2 * j) * K1) for j in range(2)]
                   for s in range(2)]
        pos_i = tile("pos_i", [P, NB * NT], i32, at + 6 * K1)
        pos_f = tile("pos_f", [P, NB * NT], f32, at + 7 * K1)
        state = tile("state", [P, HEADS_A, DV])
        k_odd = tile("k_odd", [P, 2, NT, P])
        k_even = tile("k_even", [P, 2, NT, P])
        v_odd = tile("v_odd", [P, NT, P])
        v_even = tile("v_even", [P, NT, P])
        cos = tile("cos", [P, NB * NT, HD // 2])
        sin = tile("sin", [P, NB * NT, HD // 2])
        gpost_sb = tile("gpost_sb", [P, D])
        wdecay_sb = tile("wdecay_sb", [64, HEADS_A * DK])
        const_sb = tile("const_sb", [P, sum(CONST_COLS.values())])
        cols_sb = tile("cols_sb", [P, 32])
        later_r = tile("later_r", [P, P], f32r)
        half_bm = tile("half_bm", [P, 16])
        quarter_g = tile("quarter_g", [P, 8])
        sink_sb = tile("sink_sb", [P, 16])
        no_chunk = tile("no_chunk", [P, 4, CH])
        decay_s = tile("decay_s", [P, NT, HEADS_A, 2])
        top = [tile(f"top{s}", [P, GH]) for s in range(2)]
        sink_e = [tile(f"sink_e{s}", [P, GH]) for s in range(2)]
        den = [tile(f"den{s}", [P, GH]) for s in range(2)]
        x_stat = tile("row_stat", [P, NT, 2, 6])
        x_sm = tile("row_terms", [P, 10, NT])
        o_stat = [tile(f"out_stat{j}", [P, 2, 2, 6]) for j in range(2)]
        o_sm = [tile(f"out_terms{j}", [P, 10, 2]) for j in range(2)]
        a_stat = tile("head_stat", [P, NT, 1, 6])
        a_sm = tile("head_terms", [P, 10, NT])
        ang, turns = scratch[0]
        r_abs = scratch[1][0]

        cs, col = {}, 0
        for name, n in CONST_COLS.items():
            cs[name] = const_sb[:, col:col + n]
            col += n

        pu = [ctx.enter_context(nc.psum_tensor(f"pu{b}", [P, TB], f32)) for b in range(NPB)]
        pm = [ctx.enter_context(nc.psum_tensor(f"pm{b}", [P, TB], f32)) for b in range(5)]

        def count(name, per, unit=1, done_before=0):
            return Count(ctx.enter_context(nc.semaphore(name)), per, unit, done_before)

        def plain(name):
            return ctx.enter_context(nc.semaphore(name))

        const_in = plain("const_in")
        raw_in = [count(f"raw_in{h}", NC, 16, 2) for h in range(2)]
        x_in_ok = count("x_in_ok", NT, 16)
        x_res_ok = count("x_res_ok", NT, 16)
        stored = count("stored", NT, 16, NT)
        unit_done = count("unit_done", NU)
        logits_ok = count("logits_ok", NT)
        suffix_ok = count("suffix_ok", NT)
        upd_ok = count("upd_ok", 16)
        read_ok = count("read_ok", 16)
        otr_ok = count("otr_ok", KD)
        ktr_ok = count("ktr_ok", 2)
        qtr_ok = count("qtr_ok", 8)
        score_ok = count("score_ok", 8)
        ptr_ok = count("ptr_ok", 8)
        pv_ok = count("pv_ok", 8)
        xtr_ok = count("xtr_ok", KD, done_before=KD)
        w_hi_ok = count("w_hi_ok", 2 * NC, done_before=4)
        freed_act = count("freed_act", len(FREED_BY_ACT))
        act_seq = count("act_seq", NT)
        la_hi_ok = count("la_hi_ok", NT)
        softplus_ok = count("softplus_ok", NT)
        decay_ok = count("decay_ok", NT + 1)
        v_hi_ok = count("v_hi_ok", len(V_UNITS))
        kd_hi_ok = count("kd_hi_ok", len(K_UNITS))
        oa_ok = count("oa_ok", 16)
        z_tanh_ok = count("z_tanh_ok", len(Z_UNITS))
        g_hi_ok = count("g_hi_ok", len(Z_UNITS))
        k_odd_ok = count("k_odd_ok", 2)
        q_t_ok = count("q_t_ok", 8)
        p_exp_ok = count("p_exp_ok", 16)
        pt_even_ok = count("pt_even_ok", 8)
        ob_ok = count("ob_ok", 8)
        y_hi_ok = count("y_hi_ok", KD)
        h_hi_ok = count("h_hi_ok", KD, done_before=KD)
        trig_ok = plain("trig_ok")
        later_ok = plain("later_ok")
        x_tile_ok = [plain(f"x_tile_ok{t}") for t in range(NT)]
        x_square_ok = plain("x_square_ok")
        x_norm_act_ok = plain("x_norm_act_ok")
        w_lo_dve_ok = count("w_lo_dve_ok", len(DVE_HALVES), done_before=1)
        freed_dve = count("freed_dve", len(FREED_BY_DVE))
        RSTD_LINKS = 4 + 2 + 3 * NEWTON
        ROW_LINKS = 1 + RSTD_LINKS
        dve_seq = count("dve_seq", (3 + HEADS_A) * ROW_LINKS + 2 + 6 * 8 + 4,
                        done_before=RSTD_LINKS - 4 + 2)
        abs_ok = count("abs_ok", NT)
        log_a_ok = count("log_a_ok", NT)
        la_lo_ok = count("la_lo_ok", NT)
        state_ok = count("state_ok", 32)
        oa_norm_ok = count("oa_norm_ok", NT * HEADS_A)
        gated_ok = count("gated_ok", len(Z_UNITS))
        k_even_ok = count("k_even_ok", 3)
        v_even_ok = count("v_even_ok", 1)
        shift_ok = count("shift_ok", 8)
        sink_d_ok = count("sink_d_ok", 8)
        p_norm_ok = count("p_norm_ok", 8)
        pt_odd_ok = count("pt_odd_ok", 8)
        x_norm_ok = count("x_norm_ok", NT, done_before=2)
        y_sum_ok = count("y_sum_ok", KD)
        o_scaled_ok = count("o_scaled_ok", NT)
        o_dve_ok = count("o_dve_ok", 2)
        h_lo_ok = count("h_lo_ok", KD, done_before=KD)
        prep_ok = plain("prep_ok")
        x_rstd_ok = plain("x_rstd_ok")
        w_lo_ok = count("w_lo_ok", len(POOL_HALVES), done_before=3)
        scratch_free = count("scratch_free", len(SCRATCH_USERS))
        y_lo_ok = count("y_lo_ok", KD)
        o_pool_ok = count("o_pool_ok", 2)
        zeroed = plain("zeroed")

        ACT_COUNTS = [la_hi_ok, w_hi_ok, freed_act, act_seq, softplus_ok, decay_ok, v_hi_ok, kd_hi_ok,
                      oa_ok, z_tanh_ok, g_hi_ok, k_odd_ok, q_t_ok, p_exp_ok,
                      pt_even_ok, ob_ok, y_hi_ok, h_hi_ok]
        DVE_COUNTS = [la_lo_ok, w_lo_dve_ok, freed_dve, dve_seq, abs_ok, log_a_ok, state_ok, oa_norm_ok, gated_ok,
                      k_even_ok, v_even_ok, shift_ok, sink_d_ok, p_norm_ok, pt_odd_ok,
                      x_norm_ok, y_sum_ok, o_scaled_ok, o_dve_ok, h_lo_ok]
        PE_COUNTS = [unit_done, logits_ok, suffix_ok, upd_ok, read_ok, otr_ok, ktr_ok, qtr_ok,
                     score_ok, ptr_ok, pv_ok, xtr_ok]
        POOL_COUNTS = [w_lo_ok, scratch_free, y_lo_ok, o_pool_ok, stored]
        SP_COUNTS = raw_in + [x_in_ok, x_res_ok]

        def w_half_no(c, half):
            return 2 * c + half - 3

        def lo_part(c, half):
            made = (c + NC if c < 2 else c, half)
            halves, owner = (DVE_HALVES, w_lo_dve_ok) if made in DVE_HALVES else (POOL_HALVES, w_lo_ok)
            return owner, halves.index(made) + 1 - (len(halves) if c < 2 else 0)

        def as_f32(ap):
            return ap.bitcast(f32)

        block = ctx.enter_context(nc.Block())

        @block.sync
        def _(sp):
            for c in SP_COUNTS:
                c.credit(sp)

            def load_w(c, half):
                sp.dma_start(w_raw[half][:, :, :], w[c, :, half * (KD // 2):(half + 1) * (KD // 2), :]) \
                  .then_inc(raw_in[half].sem, 16)

            def load_x(dst, at, c):
                for t in range(NT):
                    sp.dma_start(dst[:, t, :], x[ds(at + t * P, P), :]).then_inc(c.sem, 16)

            for dst, src in ((const_sb, consts), (cols_sb, cols), (pos_i, pos)):
                sp.dma_start(dst[:, :], src).then_inc(const_in, 16)
            for t in range(NT):
                sp.dma_start(x_in[:, t, :], x[ds(t * P, P), :]).then_inc(x_tile_ok[t], 16)
            for half in range(2):
                load_w(0, half)
            for half in range(2):
                own, n = lo_part(NC, half)
                sp.wait_ge(own.sem, own.at(-1, n))
                load_w(1, half)
            with sp.Fori(0, NB) as i:
                for c in range(2, NC + 2):
                    for half in range(2):
                        own, n = lo_part(c - 1, half)
                        sp.wait_ge(own.sem, own.at(i, n))
                        load_w(c % NC, half)
                    if c == 32:
                        sp.wait_ge(pv_ok.sem, pv_ok.at(i, 8))
                        load_x(x_in, ((i + 1) % NB) * TB, x_in_ok)
                    if c == 39:
                        sp.wait_ge(unit_done.sem, unit_done.at(i, unit_no(75)))
                        load_x(x_res, i * TB, x_res_ok)
            for c in raw_in + [x_in_ok, x_res_ok, stored]:
                sp.wait_ge(c.sem, c.at(NB - 1, c.per))

        @block.tensor
        def _(pe):
            for c in PE_COUNTS:
                c.credit(pe)
            mm, tr = nc.tensor.matmul, nc.tensor.transpose

            def passes(a_hi, a_lo, b_hi, b_lo):
                return ((a_hi, b_hi), (a_hi, b_lo), (a_lo, b_hi))

            def x_transpose(i, k):
                if k >= 4:
                    pe.wait_ge(h_lo_ok.sem, h_lo_ok.at(i, k - 3))
                for t in range(NT):
                    last = tr(pm[k % 4][:, t * P:(t + 1) * P], x_in[:, t, k * P:(k + 1) * P], cs["ident"])
                last.then_inc(xtr_ok.sem, 1)

            def unit(i, u):
                kind, idx, j = UNIT_AT[u]
                c = u // 2
                bank = pu[u % NPB]
                if j == 0:
                    for half in range(2):
                        own, n = lo_part(c, half)
                        pe.wait_ge(own.sem, own.at(i, n))
                prev = u - NPB
                if prev == 1:
                    prev = 1 - NPB
                back = prev < 0
                prev %= SLOTS
                own, c_free = ((FREED_BY_ACT, freed_act) if prev in FREED_BY_ACT
                               else (FREED_BY_DVE, freed_dve))
                pe.wait_ge(c_free.sem, c_free.at(i, own.index(prev) + 1 - (len(own) if back else 0)))
                if kind in ("yA", "yB"):
                    if idx == 0 and j == 0:
                        pe.wait_ge(scratch_free.sem, scratch_free.at(i, scratch_no(31 if kind == "yA" else 59)))
                    a_hi, a_lo = g_hi, g_lo
                elif kind == "out":
                    a_hi, a_lo = y_hi, y_lo
                else:
                    a_hi, a_lo = h_hi, h_lo
                wh, wl = w_hi[c % 2], w_lo[c % 2]
                if kind in TOKEN_MAJOR:
                    for t in (2 * j, 2 * j + 1):
                        for k in range(KD):
                            if u == OUT_UNITS[0] and t == 0:
                                pe.wait_ge(y_lo_ok.sem, y_lo_ok.at(i, k + 1))
                            for n, (a, b) in enumerate(passes(a_hi, a_lo, wh, wl)):
                                last = mm(bank[:, (t % 2) * CW:(t % 2 + 1) * CW],
                                          a[:, k, t * P:(t + 1) * P], b[:, k, :],
                                          start=(k == 0 and n == 0), stop=(k == KD - 1 and n == 2))
                elif kind == "lr":
                    for k in range(KD):
                        pe.wait_ge(h_lo_ok.sem, h_lo_ok.at(i, k + 1 - KD))
                        for n, a in enumerate((a_hi, a_lo)):
                            last = mm(bank[:, :], wh[:, k, 0:P], a[:, k, :],
                                      start=(k == 0 and n == 0), stop=(k == KD - 1 and n == 1))
                else:
                    for k in range(KD):
                        for n, (b, a) in enumerate(passes(wh, wl, a_hi, a_lo)):
                            last = mm(bank[:, :], b[:, k, j * P:(j + 1) * P], a[:, k, :],
                                      start=(k == 0 and n == 0), stop=(k == KD - 1 and n == 2))
                last.then_inc(unit_done.sem, 1)

            def logits(i, t):
                pe.wait_ge(freed_act.sem, freed_act.at(i, 1))
                if t == 3:
                    pe.wait_ge(log_a_ok.sem, log_a_ok.at(i, 1))
                mm(pm[LOGIT_BANK[t]][:, :], lr_t[0:64, t * P:(t + 1) * P], wdecay_sb[:, :],
                   start=True, stop=True).then_inc(logits_ok.sem, 1)

            def suffix(i, t):
                pe.wait_ge(la_lo_ok.sem, la_lo_ok.at(i, t + 1))
                if t >= 2:
                    pe.wait_ge(decay_ok.sem, decay_ok.at(i, t - 1))
                g = log_a[t % 2]
                for m, a in enumerate((la_hi, la_lo)):
                    mm(pm[SUFFIX_BANK[t]][:, :], later_r[:, :], a[t % 2][:, :], start=(m == 0), stop=(m == 1))
                for h in range(HEADS_A):
                    o = (t * HEADS_A + h) * 2
                    last = mm(pm[2][:, o:o + 2], g[:, h * DK:(h + 1) * DK], cs["chunk_of"],
                              start=True, stop=True)
                last.then_inc(suffix_ok.sem, 1)

            def update(i, n):
                h, t = divmod(n, NT)
                if t % 2 == 0:
                    pe.wait_ge(freed_dve.sem, freed_dve.at(i, dve_no(V_UNITS[2 * h + t // 2])))
                    pe.wait_ge(scratch_free.sem, scratch_free.at(i, scratch_no(K_UNITS[2 * (h // 2) + t // 2])))
                if n == 0:
                    pe.wait_ge(decay_ok.sem, decay_ok.at(i, NT + 1))
                else:
                    pe.wait_ge(state_ok.sem, state_ok.at(i, 2 * n))
                for m, (a, b) in enumerate(passes(kd_hi, kd_lo, v_hi[h % 2], v_lo[h % 2])):
                    for c in range(2):
                        r = slice(c * CH, (c + 1) * CH)
                        last = mm(pm[c][:, 0:DV], a[r, t, (h % 2) * DK:(h % 2 + 1) * DK], b[r, t, :],
                                  start=(m == 0), stop=(m == 2))
                last.then_inc(upd_ok.sem, 1)

            def read_state(i, n):
                h, t = divmod(n, NT)
                pe.wait_ge(state_ok.sem, state_ok.at(i, 2 * n + 2))
                if t == 0:
                    pe.wait_ge(freed_act.sem, freed_act.at(i, act_no(Q_UNITS[h])))
                if n:
                    pe.wait_ge(oa_ok.sem, oa_ok.at(i, n))
                for c, s in enumerate((s_mid[:, :], state[:, h, :])):
                    tok = slice(t * P + c * CH, t * P + (c + 1) * CH)
                    last = mm(pm[2][c * CH:(c + 1) * CH, 0:DV], q_a[h // 2][:, h % 2, tok], s,
                              start=True, stop=True)
                last.then_inc(read_ok.sem, 1)

            def o_transpose(i, e):
                pe.wait_ge(oa_norm_ok.sem, oa_norm_ok.at(i, NT * (e // 2 + 1)))
                if e == 6:
                    pe.wait_ge(oa_ok.sem, oa_ok.at(i, 16))
                elif e >= 2:
                    pe.wait_ge(gated_ok.sem, gated_ok.at(i, e - 1))
                for t in range(NT):
                    last = tr(pm[OTR_BANK[e]][:, t * P:(t + 1) * P], oa[:, t, e * P:(e + 1) * P],
                              cs["ident"])
                last.then_inc(otr_ok.sem, 1)

            def k_transpose(i):
                pe.wait_ge(scratch_free.sem, scratch_free.at(i, scratch_no(25)))
                pe.wait_ge(state_ok.sem, state_ok.at(i, 32))
                for g in range(2):
                    for t in range(NT):
                        last = tr(pm[g][:, t * P:(t + 1) * P],
                                  k_rope[:, t, g, :, :].rearrange("p a b -> p (a b)"), cs["ident"])
                    last.then_inc(ktr_ok.sem, 1)

            def q_transpose(i, s):
                g, t = divmod(s, NT)
                if t == 0:
                    pe.wait_ge(scratch_free.sem, scratch_free.at(i, scratch_no(29 + 6 * g)))
                if s == 0:
                    pe.wait_ge(gated_ok.sem, gated_ok.at(i, 6))
                else:
                    pe.wait_ge(q_t_ok.sem, q_t_ok.at(i, s))
                for e in range(4):
                    last = tr(pm[4][:, e * P:(e + 1) * P],
                              q_rope[:, t, (4 * g + e) * P:(4 * g + e + 1) * P], cs["ident"])
                last.then_inc(qtr_ok.sem, 1)

            def scores_wait(i, s):
                pe.wait_ge(q_t_ok.sem, q_t_ok.at(i, s + 1))
                if s == 0:
                    pe.wait_ge(k_even_ok.sem, k_even_ok.at(i, 3))
                    pe.wait_ge(k_odd_ok.sem, k_odd_ok.at(i, 2))
                    pe.wait_ge(gated_ok.sem, gated_ok.at(i, 7))
                    mm(pm[1][:, 0:2], cs["ident"], cs["chunk_of"], start=True, stop=True)
                else:
                    pe.wait_ge(pt_even_ok.sem, pt_even_ok.at(i, s))
                    pe.wait_ge(pt_odd_ok.sem, pt_odd_ok.at(i, s))

            def scores(i, s):
                g, t = divmod(s, NT)
                q = q_t[s % 2]
                for e in range(4):
                    for par in range(2):
                        dims = slice(par * HD, (par + 1) * HD)
                        for c, keys in enumerate((k_even, k_odd)):
                            rows_ = slice(c * CH, (c + 1) * CH)
                            last = mm(pm[1 + par][rows_, e * P:(e + 1) * P],
                                      q[dims, e, rows_], keys[dims, g, t, :],
                                      start=True, stop=True)
                last.then_inc(score_ok.sem, 1)

            def p_transpose(i, s):
                pe.wait_ge(p_norm_ok.sem, p_norm_ok.at(i, s + 1))
                for hh in range(GH):
                    last = tr(pm[1 + hh // 4][:, (hh % 4) * P:(hh % 4 + 1) * P],
                              prob[s % 2][:, hh, :], cs["ident"])
                last.then_inc(ptr_ok.sem, 1)

            def p_times_v(i, s):
                g, t = divmod(s, NT)
                pe.wait_ge(pt_even_ok.sem, pt_even_ok.at(i, s + 1))
                pe.wait_ge(pt_odd_ok.sem, pt_odd_ok.at(i, s + 1))
                if s == 0:
                    pe.wait_ge(v_even_ok.sem, v_even_ok.at(i, 1))
                    pe.wait_ge(gated_ok.sem, gated_ok.at(i, 8))
                else:
                    pe.wait_ge(ob_ok.sem, ob_ok.at(i, s))
                for c, v in enumerate((v_even, v_odd)):
                    for par in range(2):
                        o = pm[3][par * HD:(par + 1) * HD, :].rearrange("p (e q) -> p e q", e=4)
                        last = mm(o[:, :, c * CH:(c + 1) * CH], v[:, t, g * HD:(g + 1) * HD],
                                  prob_t[:, par * 4:(par + 1) * 4, c * CH:(c + 1) * CH],
                                  start=True, stop=True)
                last.then_inc(pv_ok.sem, 1)

            pe.wait_ge(const_in, 48)
            pe.wait_ge(x_norm_ok.sem, x_norm_ok.at(-1, NT))
            pe.wait_ge(x_norm_act_ok, 2)
            for k in range(KD):
                x_transpose(-1, k)
            pe.wait_ge(zeroed, 4)
            pe.wait_ge(later_ok, 1)
            pe.wait_ge(stored.sem, stored.at(-1, NT))
            with pe.Fori(0, NB) as i:
                for u in range(SLOTS):
                    if u in LOGITS:
                        for t in LOGITS[u]:
                            logits(i, t)
                    if u in SUFFIX:
                        for t in SUFFIX[u]:
                            suffix(i, t)
                    if u in UPD:
                        update(i, UPD[u])
                    if u in READ:
                        read_state(i, READ[u])
                    if u in OTR:
                        o_transpose(i, OTR[u])
                    if u == KTR:
                        k_transpose(i)
                    if u in PTR:
                        p_transpose(i, PTR[u])
                    if u in QTR:
                        q_transpose(i, QTR[u])
                    if u in SCORE:
                        scores_wait(i, SCORE[u])
                    if u in PV:
                        p_times_v(i, PV[u])
                    if u in SCORE:
                        scores(i, SCORE[u])
                    if u in XTR:
                        if XTR[u][0] == 0:
                            pe.wait_ge(x_norm_ok.sem, x_norm_ok.at(i, NT))
                            pe.wait_ge(ob_ok.sem, ob_ok.at(i, 8))
                        for k in XTR[u]:
                            x_transpose(i, k)
                    if u in UNIT_AT:
                        unit(i, u)

        @block.scalar
        def _(act):
            for c in ACT_COUNTS:
                c.credit(act)
            A = nc.scalar.activation
            seq = {"n": 0}

            def link(i, ins):
                seq["n"] += 1
                ins.then_inc(act_seq.sem, 1)
                act.wait_ge(act_seq.sem, act_seq.at(i, seq["n"]))

            def split_w(i, c, half):
                act.wait_ge(raw_in[half].sem, raw_in[half].at(i, c - 1))
                act.wait_ge(unit_done.sem, unit_done.at(i, unit_no(2 * c - 3) if c > 2 else c - 1))
                ks = slice(half * (KD // 2), (half + 1) * (KD // 2))
                A(w_hi[c % 2][:, ks, :], w_raw[half][:, :, :], ACT.Copy).then_inc(w_hi_ok.sem, 1)

            def x_split(i, k):
                act.wait_ge(xtr_ok.sem, xtr_ok.at(i, k + 1))
                A(h_hi[:, k, :], pm[k % 4][:, :], ACT.Copy, scale=cols_sb[:, k:k + 1]) \
                    .then_inc(h_hi_ok.sem, 1)

            for t in range(NT):
                act.wait_ge(x_tile_ok[t], 16)
                A(rows[:, t, :], x_in[:, t, :], ACT.Square, accum_out=x_sm[:, 8, t:t + 1]) \
                    .then_inc(x_square_ok, 1)
            for half in range(2):
                split_w(-1, NC, half)
            act.wait_ge(x_rstd_ok, 1)
            for t in (2, 3):
                A(x_in[:, t, :], x_in[:, t, :], ACT.Copy, scale=x_sm[:, 5, t:t + 1]) \
                    .then_inc(x_norm_act_ok, 1)
            act.wait_ge(const_in, 48)
            A(later_r[:, :], cs["later"], ACT.Copy).then_inc(later_ok, 1)
            for k in range(KD):
                x_split(-1, k)
                if k % 4 == 3:
                    split_w(-1, NC + 1, k // 4)
            act.wait_ge(prep_ok, ROPE_PREP)
            A(sin[:, :, :].rearrange("p a b -> p (a b)"), ang[:, :], ACT.Sin).then_inc(trig_ok, 1)
            A(cos[:, :, :].rearrange("p a b -> p (a b)"), r_abs[:, :], ACT.Sin, scale=-1.0,
              bias=cs["half_pi"]).then_inc(trig_ok, 1)

            with act.Fori(0, NB) as i:
                seq["n"] = 0
                for u in range(SLOTS):
                    if u >= 2:
                        split_w(i, u // 2 + 1, u % 2)
                    if u in LOGITS:
                        for t in LOGITS[u]:
                            act.wait_ge(abs_ok.sem, abs_ok.at(i, t + 1))
                            link(i, A(soft[t % 2][:, :], soft[t % 2][:, :], ACT.Exp, scale=-1.0))
                        for t in LOGITS[u]:
                            A(soft[t % 2][:, :], soft[t % 2][:, :], ACT.Ln, bias=cs["one"]) \
                                .then_inc(softplus_ok.sem, 1)
                        for t in LOGITS[u]:
                            act.wait_ge(log_a_ok.sem, log_a_ok.at(i, t + 1))
                            if t >= 2:
                                act.wait_ge(suffix_ok.sem, suffix_ok.at(i, t - 1))
                            A(la_hi[t % 2][:, :], log_a[t % 2][:, :], ACT.Copy).then_inc(la_hi_ok.sem, 1)
                    if u in SUFFIX:
                        for t in SUFFIX[u]:
                            act.wait_ge(suffix_ok.sem, suffix_ok.at(i, t + 1))
                            A(decay_w[:, t, :], pm[SUFFIX_BANK[t]][:, :], ACT.Exp, scale=1.0 / TAU) \
                                .then_inc(decay_ok.sem, 1)
                            if t == NT - 1:
                                A(decay_s[:, :, :, :].rearrange("p a b c -> p (a b c)"),
                                  pm[2][:, 0:NT * HEADS_A * 2], ACT.Exp, scale=1.0 / TAU) \
                                    .then_inc(decay_ok.sem, 1)
                    if u in READ:
                        h, t = divmod(READ[u], NT)
                        act.wait_ge(read_ok.sem, read_ok.at(i, READ[u] + 1))
                        if READ[u] == 0:
                            act.wait_ge(stored.sem, stored.at(i, 0))
                        A(oa[:, t, h * DV:(h + 1) * DV], pm[2][:, 0:DV], ACT.Copy).then_inc(oa_ok.sem, 1)
                    if u == KTR:
                        for g in range(2):
                            act.wait_ge(ktr_ok.sem, ktr_ok.at(i, g + 1))
                            if g == 0:
                                act.wait_ge(k_even_ok.sem, k_even_ok.at(i, 1))
                            A(k_odd[:, g, :, :].rearrange("p a b -> p (a b)"), pm[g][:, :], ACT.Copy) \
                                .then_inc(k_odd_ok.sem, 1)
                    if u in PTR:
                        s = PTR[u]
                        act.wait_ge(ptr_ok.sem, ptr_ok.at(i, s + 1))
                        act.wait_ge(pv_ok.sem, pv_ok.at(i, s))
                        A(prob_t[:, 0:4, :].rearrange("p a b -> p (a b)"), pm[1][:, :], ACT.Copy) \
                            .then_inc(pt_even_ok.sem, 1)
                    if u in QTR:
                        s = QTR[u]
                        act.wait_ge(qtr_ok.sem, qtr_ok.at(i, s + 1))
                        if s >= 2:
                            act.wait_ge(score_ok.sem, score_ok.at(i, s - 1))
                        A(q_t[s % 2][:, :, :].rearrange("p a b -> p (a b)"), pm[4][:, :], ACT.Copy) \
                            .then_inc(q_t_ok.sem, 1)
                    if u in PV:
                        s = PV[u]
                        g, t = divmod(s, NT)
                        act.wait_ge(pv_ok.sem, pv_ok.at(i, s + 1))
                        A(ob[:, 4 * g:4 * g + 4, t * P:(t + 1) * P],
                          pm[3][:, :].rearrange("p (e q) -> p e q", e=4), ACT.Copy).then_inc(ob_ok.sem, 1)
                    if u in SCORE:
                        s = SCORE[u]
                        act.wait_ge(shift_ok.sem, shift_ok.at(i, s + 1))
                        A(prob[s % 2][:, :, :], prob[s % 2][:, :, :], ACT.Exp).then_inc(p_exp_ok.sem, 1)
                        act.wait_ge(sink_d_ok.sem, sink_d_ok.at(i, s + 1))
                        A(sink_e[s % 2][:, :], sink_e[s % 2][:, :], ACT.Exp).then_inc(p_exp_ok.sem, 1)
                    if u in XTR:
                        for k in XTR[u]:
                            x_split(i, k)
                    if u - 1 in Z_UNITS:
                        _, idx, j = UNIT_AT[u - 1]
                        act.wait_ge(gated_ok.sem, gated_ok.at(i, Z_UNITS.index(u - 1) + 1))
                        A(g_hi[:, 2 * idx + j, :], scratch[SCRATCH_USERS.index(u - 1) % 2][0][:, :],
                          ACT.Copy).then_inc(g_hi_ok.sem, 1)
                    if u == SLOTS - 1:
                        for half in range(2):
                            split_w(i, NC + 1, half)
                    for e in Y_SPLIT.get(u, ()):
                        act.wait_ge(y_sum_ok.sem, y_sum_ok.at(i, e + 1))
                        A(y_hi[:, e, :], y_sum[:, e, :], ACT.Copy).then_inc(y_hi_ok.sem, 1)
                    if u not in UNIT_AT:
                        continue
                    kind, idx, j = UNIT_AT[u]
                    bank = pu[u % NPB]
                    if kind in ("kA", "zA", "zB"):
                        pair = scratch[SCRATCH_USERS.index(u) % 2]
                    if kind != "kA" and kind not in ("yA", "yB", "kvB", "qB"):
                        act.wait_ge(unit_done.sem, unit_done.at(i, unit_no(u)))
                    if kind == "lr":
                        A(lr_t[0:64, :], bank[0:64, :], ACT.Identity, bias=cs["bias_row"][0:64, :]) \
                            .then_inc(freed_act.sem, 1)
                    elif kind == "vA":
                        A(v_hi[idx % 2][:, 2 * j:2 * j + 2, :].rearrange("p a b -> p (a b)"), bank[:, :],
                          ACT.Copy).then_inc(v_hi_ok.sem, 1)
                    elif kind == "qA":
                        A(q_a[idx][:, j, :], bank[:, :], ACT.Copy, scale=DK ** -0.5) \
                            .then_inc(freed_act.sem, 1)
                    elif kind == "kA":
                        act.wait_ge(freed_dve.sem, freed_dve.at(i, dve_no(u)))
                        if idx:
                            act.wait_ge(upd_ok.sem, upd_ok.at(i, 2 * (j + 1) + NT))
                        A(kd_hi[:, 2 * j:2 * j + 2, :].rearrange("p a b -> p (a b)"), pair[0][:, :],
                          ACT.Copy).then_inc(kd_hi_ok.sem, 1)
                    elif kind in ("zA", "zB"):
                        act.wait_ge(scratch_free.sem, scratch_free.at(i, scratch_no(u) - 2))
                        A(pair[0][:, :], bank[:, :], ACT.Tanh, scale=0.5).then_inc(z_tanh_ok.sem, 1)
                    elif kind in ("mA", "mB"):
                        m = M_UNITS.index(u)
                        if m >= 12:
                            act.wait_ge(y_sum_ok.sem, y_sum_ok.at(i, m - 11))
                        elif m >= 4:
                            act.wait_ge(freed_dve.sem, freed_dve.at(i, dve_no(M_UNITS[m - 4] + 2)))
                        A(gate[m % 4][:, :], bank[:, :], ACT.Tanh, scale=0.5,
                          bias=half_bm[:, m:m + 1]).then_inc(freed_act.sem, 1)
                    elif kind == "out":
                        if u == OUT_UNITS[0]:
                            act.wait_ge(y_lo_ok.sem, y_lo_ok.at(i, KD))
                        A(rows[:, 2 * j:2 * j + 2, idx * CW:(idx + 1) * CW],
                          bank[:, :].rearrange("p (a b) -> p a b", a=2), ACT.Copy) \
                            .then_inc(freed_act.sem, 1)
            assert seq["n"] == act_seq.per, seq

        @block.vector
        def _(dve):
            for c in DVE_COUNTS:
                c.credit(dve)
            V = nc.vector
            seq = {"n": 0}

            def link(i, ins):
                seq["n"] += 1
                ins.then_inc(dve_seq.sem, 1)
                dve.wait_ge(dve_seq.sem, dve_seq.at(i, seq["n"]))

            def split_w(i, c, half):
                if (c, half) not in DVE_HALVES:
                    return
                dve.wait_ge(w_hi_ok.sem, w_hi_ok.at(i, w_half_no(c, half)))
                ks = slice(half * (KD // 2), (half + 1) * (KD // 2))
                V.tensor_tensor(w_lo[c % 2][:, ks, :], w_raw[half][:, :, :], as_f32(w_hi[c % 2][:, ks, :]),
                                ALU.subtract).then_inc(w_lo_dve_ok.sem, 1)

            def row_stats(i, stat, src, t, half):
                ins = V.bn_stats(stat[:, t, half, :], src[:, t, half * 512:(half + 1) * 512])
                if t == NT - 1 and half:
                    link(i, ins)

            def row_mean(i, stat, sm, width):
                tiles = stat.shape[1]
                v = stat[:, :, :, :].rearrange("p t h (e c) -> p (t h e) c", c=3)
                flat = sm[:, :, :].rearrange("p a b -> p (a b)")
                n = v.shape[1]
                link(i, V.tensor_tensor(flat[:, 0:n], v[:, :, 1], v[:, :, 1], ALU.mult))
                link(i, V.scalar_tensor_tensor(flat[:, n:2 * n], flat[:, 0:n], float(width * tiles // n),
                                               v[:, :, 2], ALU.mult, ALU.add))
                link(i, V.reduce_sum(sm[:, 8, :], flat[:, n:2 * n].rearrange("p (t e) -> p t e", t=tiles),
                                     AX.X))
                link(i, V.tensor_scalar(sm[:, 9, :], sm[:, 8, :], 1.0 / width, EPS, ALU.mult, ALU.add))

            def row_rstd(i, sm, done=None):
                bits = sm[:, :, :].bitcast(i32)
                link(i, V.tensor_scalar(bits[:, 0, :], bits[:, 9, :], 1, None, ALU.arith_shift_right))
                link(i, V.tensor_scalar(bits[:, 5, :], bits[:, 0, :], -1, 0x5F3759DF, ALU.mult, ALU.add))
                for step in range(NEWTON):
                    link(i, V.scalar_tensor_tensor(sm[:, 2, :], sm[:, 5, :], -0.5, sm[:, 9, :],
                                                   ALU.mult, ALU.mult))
                    link(i, V.tensor_tensor(sm[:, 3, :], sm[:, 2, :], sm[:, 5, :], ALU.mult))
                    ins = V.scalar_tensor_tensor(sm[:, 5, :], sm[:, 3, :], 1.5, sm[:, 5, :],
                                                 ALU.add, ALU.mult)
                    if done is not None and step == NEWTON - 1:
                        ins.then_inc(done, 1)
                    else:
                        link(i, ins)

            def add_rows(i, j):
                dve.wait_ge(x_res_ok.sem, x_res_ok.at(i, NT))
                dve.wait_ge(o_scaled_ok.sem, o_scaled_ok.at(i, 2 * j + 2))
                r = rows[:, 2 * j + 1, :]
                V.tensor_tensor(r, r, x_res[:, 2 * j + 1, :], ALU.add).then_inc(o_dve_ok.sem, 1)

            def x_norm(i, t):
                V.tensor_scalar(x_in[:, t, :], x_in[:, t, :], x_sm[:, 5, t:t + 1], None, ALU.mult) \
                    .then_inc(x_norm_ok.sem, 1)

            def x_split(i, k):
                dve.wait_ge(h_hi_ok.sem, h_hi_ok.at(i, k + 1))
                V.scalar_tensor_tensor(h_lo[:, k, :], pm[k % 4][:, :], cols_sb[:, k:k + 1],
                                       as_f32(h_hi[:, k, :]), ALU.mult, ALU.subtract) \
                    .then_inc(h_lo_ok.sem, 1)

            a3 = ang[:, :].rearrange("p (t f) -> p t f", t=NB * NT)
            magic = float(1.5 * 2 ** 23)

            prep = {"n": 0}

            def step(ins):
                prep["n"] += 1
                ins.then_inc(prep_ok, 1)
                dve.wait_ge(prep_ok, prep["n"])

            def whole_turns(scale):
                step(V.tensor_scalar(turns[:, :], ang[:, :], float(1 / (2 * np.pi * scale)), magic,
                                     ALU.mult, ALU.add))
                step(V.tensor_scalar(turns[:, :], turns[:, :], -magic, scale, ALU.add, ALU.mult))

            def take_turns(parts):
                for part in parts:
                    step(V.scalar_tensor_tensor(ang[:, :], turns[:, :], -part, ang[:, :],
                                                ALU.mult, ALU.add))

            parts = two_pi_parts(6)

            seq["n"] = dve_seq.per - dve_seq.done_before
            dve.wait_ge(const_in, 48)
            step(V.tensor_copy(pos_f[:, :], pos_i[:, :]))
            step(V.tensor_tensor(a3, pos_f[:, :].unsqueeze(2).broadcast_to([P, NB * NT, HD // 2]),
                                 cs["inv_freq"].unsqueeze(1).broadcast_to([P, NB * NT, HD // 2]), ALU.mult))
            whole_turns(4096.0)
            take_turns(parts)
            whole_turns(1.0)
            take_turns(parts[0:1])
            dve.wait_ge(x_square_ok, NT)
            link(-1, V.tensor_scalar(x_sm[:, 9, :], x_sm[:, 8, :], 1.0 / D, EPS, ALU.mult, ALU.add))
            row_rstd(-1, x_sm, x_rstd_ok)
            dve.wait_ge(x_rstd_ok, 1)
            for t in range(2):
                x_norm(-1, t)
            take_turns(parts[1:3])
            for k in range(KD):
                x_split(-1, k)
            split_w(-1, NC + 1, 1)
            take_turns(parts[3:6])
            step(V.tensor_scalar(ang[:, :], ang[:, :], 3.1415925, -3.1415925, ALU.min, ALU.max))
            step(V.scalar_tensor_tensor(r_abs[:, :], ang[:, :], -1.0, ang[:, :], ALU.mult, ALU.max))
            assert prep["n"] == ROPE_PREP
            link(-1, V.tensor_scalar(quarter_g[:, :], cols_sb[:, 8:16], 0.25, None, ALU.mult))
            seq["n"] += 1
            assert seq["n"] == dve_seq.per, seq
            V.tensor_scalar(half_bm[:, :], cols_sb[:, 16:32], 0.5, None, ALU.mult) \
                .then_inc(dve_seq.sem, 1)
            dve.wait_ge(stored.sem, stored.at(-1, NT))
            dve.wait_ge(trig_ok, 2)
            dve.wait_ge(zeroed, 4)

            def rope(i, u):
                kind, idx, j = UNIT_AT[u]
                heads = 2 if kind == "kvB" else CW // HD
                r_cos, r_sin = scratch[SCRATCH_USERS.index(u) % 2]
                for a in range(2):
                    o = pu[u % NPB][:, a * CW:a * CW + heads * HD].rearrange("p (h e) -> p h e", e=HD // 2)
                    oh = pu[u % NPB][:, a * CW:a * CW + heads * HD] \
                        .rearrange("p (h x e) -> p h x e", x=2, e=HD // 2)
                    dst = slice(a * CW, a * CW + heads * HD)
                    table = ds(i * NT + (2 * j + a), 1)
                    V.tensor_tensor(r_cos[:, dst].rearrange("p (h e) -> p h e", e=HD // 2), o,
                                    cos[:, table, :].broadcast_to([P, 2 * heads, HD // 2]), ALU.mult)
                    d = r_sin[:, dst].rearrange("p (h x e) -> p h x e", x=2, e=HD // 2)
                    for x_ in range(2):
                        last = V.tensor_tensor(d[:, :, x_, :], oh[:, :, 1 - x_, :],
                                               sin[:, table, :].broadcast_to([P, heads, HD // 2]), ALU.mult)
                return last

            with dve.Fori(0, NB) as i:
                seq["n"] = 0
                for u in range(SLOTS):
                    if u >= 2:
                        split_w(i, u // 2 + 1, u % 2)
                    if u == SLOTS - 1:
                        split_w(i, NC + 1, 1)
                        add_rows(i, 0)
                    if u in LOGITS:
                        for t in LOGITS[u]:
                            logit = pm[LOGIT_BANK[t]]
                            dve.wait_ge(logits_ok.sem, logits_ok.at(i, t + 1))
                            if t >= 2:
                                dve.wait_ge(log_a_ok.sem, log_a_ok.at(i, t - 1))
                            V.tensor_scalar(soft[t % 2][:, :].bitcast(i32), logit[:, :].bitcast(i32), 0x7FFFFFFF, None,
                                            ALU.bitwise_and) \
                                .then_inc(abs_ok.sem, 1)
                        for t in LOGITS[u]:
                            dve.wait_ge(softplus_ok.sem, softplus_ok.at(i, t + 1))
                            if t >= 2:
                                dve.wait_ge(suffix_ok.sem, suffix_ok.at(i, t - 1))
                            V.scalar_tensor_tensor(log_a[t % 2][:, :], pm[LOGIT_BANK[t]][:, :], 0.0,
                                                   soft[t % 2][:, :], ALU.min, ALU.subtract) \
                                .then_inc(log_a_ok.sem, 1)
                        for t in LOGITS[u]:
                            dve.wait_ge(la_hi_ok.sem, la_hi_ok.at(i, t + 1))
                            V.tensor_tensor(la_lo[t % 2][:, :], log_a[t % 2][:, :],
                                            as_f32(la_hi[t % 2][:, :]), ALU.subtract) \
                                .then_inc(la_lo_ok.sem, 1)
                    if u in UPD:
                        n = UPD[u]
                        h, t = divmod(n, NT)
                        dve.wait_ge(upd_ok.sem, upd_ok.at(i, n + 1))
                        if n == 0:
                            dve.wait_ge(decay_ok.sem, decay_ok.at(i, NT + 1))
                        dve.wait_ge(read_ok.sem, read_ok.at(i, n))
                        V.scalar_tensor_tensor(s_mid[:, :], state[:, h, :], decay_s[:, t, h, 0:1],
                                               pm[0][:, 0:DV], ALU.mult, ALU.add).then_inc(state_ok.sem, 1)
                        dve.wait_ge(state_ok.sem, state_ok.at(i, 2 * n + 1))
                        V.scalar_tensor_tensor(state[:, h, :], s_mid[:, :], decay_s[:, t, h, 1:2],
                                               pm[1][:, 0:DV], ALU.mult, ALU.add).then_inc(state_ok.sem, 1)
                    if u - 1 in READ:
                        h, t = divmod(READ[u - 1], NT)
                        dve.wait_ge(oa_ok.sem, oa_ok.at(i, READ[u - 1] + 1))
                        ins = V.bn_stats(a_stat[:, t, 0, :], oa[:, t, h * DV:(h + 1) * DV])
                        if t == NT - 1:
                            link(i, ins)
                            row_mean(i, a_stat, a_sm, DV)
                            row_rstd(i, a_sm)
                            for t in range(NT):
                                o = oa[:, t, h * DV:(h + 1) * DV]
                                V.tensor_scalar(o, o, a_sm[:, 5, t:t + 1], None, ALU.mult) \
                                    .then_inc(oa_norm_ok.sem, 1)
                    if u == KTR:
                        V.tensor_copy(k_even[:, :, 0, CH:P], k_odd[:, :, NT - 1, CH:P]) \
                            .then_inc(k_even_ok.sem, 1)
                        dve.wait_ge(k_odd_ok.sem, k_odd_ok.at(i, 2))
                        V.tensor_copy(k_even[:, :, :, 0:CH], k_odd[:, :, :, 0:CH]).then_inc(k_even_ok.sem, 1)
                        V.tensor_copy(k_even[:, :, 1:NT, CH:P], k_odd[:, :, 0:NT - 1, CH:P]) \
                            .then_inc(k_even_ok.sem, 1)
                    if u in PTR:
                        s = PTR[u]
                        dve.wait_ge(ptr_ok.sem, ptr_ok.at(i, s + 1))
                        dve.wait_ge(pv_ok.sem, pv_ok.at(i, s))
                        V.tensor_copy(prob_t[:, 4:8, :].rearrange("p a b -> p (a b)"), pm[2][:, :]) \
                            .then_inc(pt_odd_ok.sem, 1)
                    if u in SCORE:
                        s = SCORE[u]
                        g = s // NT
                        tp, se = top[s % 2], sink_e[s % 2]
                        dve.wait_ge(score_ok.sem, score_ok.at(i, s + 1))
                        if s % NT == 0:
                            for par in range(2):
                                early = pm[1 + par][0:CH, :].rearrange("p (e k) -> p e k", e=4)[:, :, CH:P]
                                link(i, V.tensor_tensor(early, early, no_chunk[0:CH, :, :], ALU.add))
                        for par in range(2):
                            ins = V.reduce_max(tp[:, 4 * par:4 * par + 4],
                                               pm[1 + par][:, :].rearrange("p (e k) -> p e k", e=4), AX.X)
                            link(i, ins)
                        link(i, V.scalar_tensor_tensor(tp[:, :], tp[:, :], HD ** -0.5,
                                                       sink_sb[:, 8 * g:8 * g + 8], ALU.mult, ALU.max))
                        if s >= 2:
                            dve.wait_ge(ptr_ok.sem, ptr_ok.at(i, s - 1))
                        for par in range(2):
                            ins = V.scalar_tensor_tensor(
                                prob[s % 2][:, 4 * par:4 * par + 4, :],
                                pm[1 + par][:, :].rearrange("p (e k) -> p e k", e=4), HD ** -0.5,
                                tp[:, 4 * par:4 * par + 4].unsqueeze(2).broadcast_to([P, 4, P]),
                                ALU.mult, ALU.subtract)
                        ins.then_inc(shift_ok.sem, 1)
                        V.tensor_tensor(se[:, :], sink_sb[:, 8 * g:8 * g + 8], tp[:, :], ALU.subtract) \
                            .then_inc(sink_d_ok.sem, 1)
                        if s == NT:
                            V.memset(no_chunk[:, :, :], 0.0)
                    if u - 1 in SCORE:
                        s = SCORE[u - 1]
                        dve.wait_ge(p_exp_ok.sem, p_exp_ok.at(i, 2 * s + 2))
                        link(i, V.reduce_sum(den[s % 2][:, :], prob[s % 2][:, :, :], AX.X))
                        link(i, V.tensor_tensor(den[s % 2][:, :], den[s % 2][:, :], sink_e[s % 2][:, :],
                                                ALU.add))
                        link(i, V.reciprocal(den[s % 2][:, :], den[s % 2][:, :]))
                        pr = prob[s % 2]
                        V.tensor_tensor(pr[:, :, :], pr[:, :, :],
                                        den[s % 2][:, :].unsqueeze(2).broadcast_to([P, GH, P]), ALU.mult) \
                            .then_inc(p_norm_ok.sem, 1)
                    if u in XSTAT:
                        if XSTAT[u] == 0:
                            dve.wait_ge(x_in_ok.sem, x_in_ok.at(i, NT))
                        for half in range(2):
                            row_stats(i, x_stat, x_in, XSTAT[u], half)
                    if u == XRSTD:
                        row_mean(i, x_stat, x_sm, D)
                        row_rstd(i, x_sm)
                    if u in XNORM:
                        x_norm(i, XNORM[u])
                    if u in XTR:
                        for k in XTR[u]:
                            x_split(i, k)
                    if u - 1 in Z_UNITS:
                        kind, idx, j = UNIT_AT[u - 1]
                        e = 2 * idx + j
                        pair = scratch[SCRATCH_USERS.index(u - 1) % 2]
                        dve.wait_ge(freed_dve.sem, freed_dve.at(i, dve_no(u - 1)))
                        if kind == "zA":
                            dve.wait_ge(otr_ok.sem, otr_ok.at(i, e + 1))
                            V.scalar_tensor_tensor(pair[0][:, :], pm[OTR_BANK[e]][:, :], quarter_g[:, e:e + 1],
                                                   pair[0][:, :], ALU.mult, ALU.mult) \
                                .then_inc(gated_ok.sem, 1)
                        else:
                            dve.wait_ge(ob_ok.sem, ob_ok.at(i, 4 * (e // 4) + 4))
                            V.scalar_tensor_tensor(pair[0][:, :], ob[:, e, :], 0.25, pair[0][:, :],
                                                   ALU.mult, ALU.mult).then_inc(gated_ok.sem, 1)
                    if u not in UNIT_AT:
                        continue
                    kind, idx, j = UNIT_AT[u]
                    bank = pu[u % NPB]
                    if u in SCRATCH_USERS:
                        pair = scratch[SCRATCH_USERS.index(u) % 2]
                    free = freed_dve.sem
                    if kind == "vA":
                        dve.wait_ge(v_hi_ok.sem, v_hi_ok.at(i, V_UNITS.index(u) + 1))
                        hi = v_hi[idx % 2][:, 2 * j:2 * j + 2, :].rearrange("p a b -> p (a b)")
                        V.tensor_tensor(v_lo[idx % 2][:, 2 * j:2 * j + 2, :].rearrange("p a b -> p (a b)"),
                                        bank[:, :], as_f32(hi), ALU.subtract).then_inc(free, 1)
                    elif kind == "kA":
                        dve.wait_ge(unit_done.sem, unit_done.at(i, unit_no(u)))
                        dve.wait_ge(decay_ok.sem, decay_ok.at(i, 2 * j + 2))
                        dve.wait_ge(scratch_free.sem, scratch_free.at(i, scratch_no(u) - 2))
                        V.tensor_tensor(pair[0][:, :].rearrange("p (a b) -> p a b", a=2),
                                        bank[:, :].rearrange("p (a b) -> p a b", a=2),
                                        decay_w[:, 2 * j:2 * j + 2, idx * CW:(idx + 1) * CW], ALU.mult) \
                            .then_inc(free, 1)
                    elif kind in ("zA", "zB"):
                        dve.wait_ge(z_tanh_ok.sem, z_tanh_ok.at(i, Z_UNITS.index(u) + 1))
                        V.scalar_tensor_tensor(pair[0][:, :], pair[0][:, :], 1.0, bank[:, :],
                                               ALU.add, ALU.mult).then_inc(free, 1)
                    elif kind == "yA":
                        e = 2 * idx + j
                        dve.wait_ge(freed_act.sem, freed_act.at(i, act_no(u - 2)))
                        dve.wait_ge(unit_done.sem, unit_done.at(i, unit_no(u)))
                        V.scalar_tensor_tensor(y_sum[:, e, :], gate[e % 4][:, :], 1.0, bank[:, :],
                                               ALU.add, ALU.mult).then_inc(free, 1)
                    elif kind == "yB":
                        e = 2 * idx + j
                        gt = gate[e % 4]
                        dve.wait_ge(freed_act.sem, freed_act.at(i, act_no(u - 2)))
                        dve.wait_ge(unit_done.sem, unit_done.at(i, unit_no(u)))
                        V.scalar_tensor_tensor(gt[:, :], gt[:, :], 1.0, bank[:, :],
                                               ALU.add, ALU.mult).then_inc(free, 1)
                        dve.wait_ge(freed_dve.sem, freed_dve.at(i, dve_no(u)))
                        V.tensor_tensor(y_sum[:, e, :], y_sum[:, e, :], gt[:, :], ALU.add) \
                            .then_inc(y_sum_ok.sem, 1)
                    elif kind in ("kvB", "qB"):
                        dve.wait_ge(unit_done.sem, unit_done.at(i, unit_no(u)))
                        dve.wait_ge(scratch_free.sem, scratch_free.at(i, scratch_no(u) - 2))
                        last = rope(i, u)
                        if kind == "kvB":
                            if j == 0:
                                link(i, V.tensor_copy(v_even[CH:P, 0, :], v_odd[CH:P, NT - 1, :]))
                            last = V.tensor_copy(v_odd[:, 2 * j:2 * j + 2, :],
                                                 bank[:, :].rearrange("p (a b) -> p a b", a=2)[:, :, P:2 * P])
                        last.then_inc(free, 1)
                        if kind == "kvB" and j == 1:
                            dve.wait_ge(freed_dve.sem, freed_dve.at(i, dve_no(u)))
                            link(i, V.tensor_copy(v_even[0:CH, :, :], v_odd[0:CH, :, :]))
                            V.tensor_copy(v_even[CH:P, 1:NT, :], v_odd[CH:P, 0:NT - 1, :]) \
                                .then_inc(v_even_ok.sem, 1)
                    elif kind == "out":
                        if idx % 2:
                            dve.wait_ge(freed_act.sem, freed_act.at(i, act_no(u)))
                            for t in range(2):
                                ins = V.bn_stats(o_stat[j][:, t, idx // 2, :],
                                                 rows[:, 2 * j + t, (idx // 2) * 512:(idx // 2 + 1) * 512])
                        if idx == 3:
                            link(i, ins)
                            row_mean(i, o_stat[j], o_sm[j], D)
                            row_rstd(i, o_sm[j])
                            for t in range(2):
                                r = rows[:, 2 * j + t, :]
                                V.scalar_tensor_tensor(r, r, o_sm[j][:, 5, t:t + 1], gpost_sb[:, :],
                                                       ALU.mult, ALU.mult).then_inc(o_scaled_ok.sem, 1)
                            if j == 1:
                                add_rows(i, j)
            assert seq["n"] == dve_seq.per, seq

        @block.gpsimd
        def _(pool):
            for c in POOL_COUNTS:
                c.credit(pool)
            G = nc.gpsimd
            TT = G.tensor_tensor

            def split_w(i, c, half):
                if (c, half) in DVE_HALVES:
                    return
                pool.wait_ge(w_hi_ok.sem, w_hi_ok.at(i, w_half_no(c, half)))
                ks = slice(half * (KD // 2), (half + 1) * (KD // 2))
                if c == NC:
                    own = slice(RANK, 2 * RANK)
                    TT(w_hi[0][:, ks, own], w_raw[half][:, :, own], as_f32(w_hi[0][:, ks, own]),
                       ALU.subtract).then_inc(w_lo_ok.sem, 1)
                else:
                    TT(w_lo[c % 2][:, ks, :], w_raw[half][:, :, :], as_f32(w_hi[c % 2][:, ks, :]),
                       ALU.subtract).then_inc(w_lo_ok.sem, 1)

            def add_rows(i, j):
                pool.wait_ge(x_res_ok.sem, x_res_ok.at(i, NT))
                pool.wait_ge(o_scaled_ok.sem, o_scaled_ok.at(i, 2 * j + 1))
                TT(rows[:, 2 * j, :], rows[:, 2 * j, :], x_res[:, 2 * j, :], ALU.add) \
                    .then_inc(o_pool_ok.sem, 1)

            def store_rows(i, j):
                pool.wait_ge(o_pool_ok.sem, o_pool_ok.at(i, j + 1))
                pool.wait_ge(o_dve_ok.sem, o_dve_ok.at(i, j + 1))
                for t in (2 * j, 2 * j + 1):
                    pool.dma_start(out[ds(i * TB + t * P, P), :], rows[:, t, :]).then_inc(stored.sem, 16)

            for dst, src in ((wdecay_sb[:, :], w_decay), (sink_sb[:, :], sinks),
                             (gpost_sb[:, 0:D // 2], gpost[:, 0:D // 2]),
                             (gpost_sb[:, D // 2:D], gpost[:, D // 2:D])):
                pool.dma_start(dst, src).then_inc(stored.sem, 16)
            G.memset(state[:, :, :], 0.0).then_inc(zeroed, 1)
            G.memset(k_odd[:, :, :, :], 0.0).then_inc(zeroed, 1)
            G.memset(v_odd[:, :, :], 0.0).then_inc(zeroed, 1)
            G.memset(no_chunk[:, :, :], NEG).then_inc(zeroed, 1)
            for c in (NC, NC + 1):
                for half in range(2):
                    split_w(-1, c, half)

            with pool.Fori(0, NB) as i:
                for u in range(SLOTS):
                    if u >= 2:
                        split_w(i, u // 2 + 1, u % 2)
                    if u - 1 in Z_UNITS:
                        _, idx, j = UNIT_AT[u - 1]
                        e = 2 * idx + j
                        pool.wait_ge(g_hi_ok.sem, g_hi_ok.at(i, Z_UNITS.index(u - 1) + 1))
                        TT(g_lo[:, e, :], scratch[SCRATCH_USERS.index(u - 1) % 2][0][:, :],
                           as_f32(g_hi[:, e, :]), ALU.subtract).then_inc(scratch_free.sem, 1)
                    for e in Y_SPLIT.get(u, ()):
                        pool.wait_ge(y_hi_ok.sem, y_hi_ok.at(i, e + 1))
                        TT(y_lo[:, e, :], y_sum[:, e, :], as_f32(y_hi[:, e, :]), ALU.subtract) \
                            .then_inc(y_lo_ok.sem, 1)
                    if u not in UNIT_AT:
                        continue
                    kind, idx, j = UNIT_AT[u]
                    if u in SCRATCH_USERS:
                        pair = scratch[SCRATCH_USERS.index(u) % 2]
                    done = scratch_free.sem
                    if kind == "kA":
                        pool.wait_ge(kd_hi_ok.sem, kd_hi_ok.at(i, K_UNITS.index(u) + 1))
                        rows_ = slice(2 * j, 2 * j + 2)
                        TT(kd_lo[:, rows_, :].rearrange("p a b -> p (a b)"), pair[0][:, :],
                           as_f32(kd_hi[:, rows_, :].rearrange("p a b -> p (a b)")), ALU.subtract) \
                            .then_inc(done, 1)
                    elif kind in ("kvB", "qB"):
                        pool.wait_ge(freed_dve.sem, freed_dve.at(i, dve_no(u)))
                        r_cos, r_sin = pair
                        if kind == "qB":
                            dst = q_rope[:, 2 * j:2 * j + 2, idx * CW:(idx + 1) * CW] \
                                .rearrange("p t (h x e) -> p t h x e", x=2, e=HD // 2)
                            c4, s4 = (r[:, :].rearrange("p (t h x e) -> p t h x e", t=2, x=2, e=HD // 2)
                                      for r in (r_cos, r_sin))
                            for x_, op in enumerate((ALU.subtract, ALU.add)):
                                ins = TT(dst[:, :, :, x_, :], c4[:, :, :, x_, :], s4[:, :, :, x_, :], op)
                        else:
                            for a in range(2):
                                c4, s4 = (r[:, a * CW:a * CW + 2 * HD]
                                          .rearrange("p (h x e) -> p h x e", x=2, e=HD // 2)
                                          for r in (r_cos, r_sin))
                                dst = k_rope[:, 2 * j + a, :, :, :] \
                                    .rearrange("p h c (x e) -> p h c x e", x=2)
                                for x_, op in enumerate((ALU.subtract, ALU.add)):
                                    c_, s_ = (v[:, :, x_, :].unsqueeze(2).broadcast_to([P, 2, 2, HD // 2])
                                              for v in (c4, s4))
                                    ins = TT(dst[:, :, :, x_, :], c_, s_, op)
                        ins.then_inc(done, 1)
                for half in range(2):
                    split_w(i, NC + 1, half)
                for j in range(2):
                    add_rows(i, j)
                    store_rows(i, j)


ROPE_PREP = 2 + 2 * (2 + 6) + 2


INS = ["x", "w", "w_decay", "pos", "cols", "sinks", "gpost", "consts"]


def kernel(x, positions, g_pre, w_in, w_decay_up, b_decay_up, g_gla, attn_sinks,
           w_branch_gla, w_branch_swa, b_merge, w_out, g_post):
    import concourse.bacc as bacc
    from concourse.bass_utils import run_bass_kernel_spmd as run

    w_in, wa, wb, wo = (np.asarray(a)[0] for a in (w_in, w_branch_gla, w_branch_swa, w_out))
    first = dict(qA=0, kA=512, vA=1024, lr=2048, zA=2064, qB=3088, kvB=4112, zB=4368, mA=5392, mB=6416)
    w = np.zeros((NC, P, KD, CW), np.float32)
    for c, (kind, idx) in enumerate(CHUNKS):
        src, col = {"yA": (wa, 0), "yB": (wb, 0), "out": (wo, 0)}.get(kind, (w_in, first.get(kind)))
        width = RANK if kind == "lr" else CW
        part = src[:, col + idx * CW:col + idx * CW + width]
        part = part.reshape(KD, P, width).transpose(1, 0, 2)
        w[c, :, :, :width] = part
        if kind == "lr":
            w[c, :, :, RANK:2 * RANK] = part
    w_decay = np.zeros((64, HEADS_A * DK), np.float32)
    w_decay[:2 * RANK] = np.tile(np.asarray(w_decay_up)[0], (2, 1))
    w_decay[2 * RANK] = np.asarray(b_decay_up)[0]
    cols = np.concatenate([np.asarray(a)[0].reshape(-1, P).T for a in (g_pre, g_gla, b_merge)], axis=1)
    sinks = np.asarray(attn_sinks)[0].reshape(2, 4, 2).transpose(0, 2, 1).reshape(1, 16)
    arrays = {
        "x": np.ascontiguousarray(np.asarray(x)[0]), "w": w, "w_decay": w_decay,
        "pos": np.ascontiguousarray(np.asarray(positions)[0].reshape(NB * NT, P).T),
        "cols": np.ascontiguousarray(cols), "sinks": np.ascontiguousarray(np.broadcast_to(sinks, (P, 16))),
        "gpost": np.ascontiguousarray(np.broadcast_to(np.asarray(g_post)[0], (P, D))),
        "consts": const_array(),
    }
    nc = bacc.Bacc("TRN2", target_bir_lowering=False, num_devices=1, dynamic_dma_scratch_size=768)
    args = [nc.dram_tensor(f"in_{n}", arrays[n].shape, mybir.dt.from_np(arrays[n].dtype),
                           kind="ExternalInput").ap() for n in INS]
    out = nc.dram_tensor("out_y", (SEQ, D), mybir.dt.float32, kind="ExternalOutput").ap()
    build(nc, *args, out)
    r = run(nc, [{f"in_{n}": arrays[n] for n in INS}], core_ids=[0])
    return r.results[0]["out_y"].reshape(1, SEQ, D)
```
